# Optimizing a Trainium2 kernel written in Bass

```python
import math
import jax, jax.numpy as jnp
from jax import lax
import numpy as np

D_MODEL = 1024
BATCH = 1
SEQ = 256
DEPTH = 2

CHUNK = 64
N_HEADS = 16
N_KV_HEADS = 4
HEAD_DIM = 64
GROUP = N_HEADS // N_KV_HEADS
ATTN_WIDTH = N_HEADS * HEAD_DIM
KV_WIDTH = N_KV_HEADS * HEAD_DIM
WINDOW = 128
WINDOW_CHUNKS = WINDOW // CHUNK
ROPE_THETA = 10000.0
LRU_WIDTH = D_MODEL
LRU_BLOCKS = 16
LRU_BLOCK_DIM = LRU_WIDTH // LRU_BLOCKS
CONV_WIDTH = 4
LRU_C = 8.0
D_FF = ((8 * D_MODEL // 3 + 255) // 256) * 256
IN_WIDTH = 2 * LRU_WIDTH + ATTN_WIDTH + 2 * KV_WIDTH + 2 * D_MODEL
EPS = 1e-6
NEG_INF = -1e30

kernel_name = "hawk_swa_sink_parallel_hybrid"

def rmsnorm(x, g):
    xf = x.astype(jnp.float32)
    y = xf * lax.rsqrt(jnp.mean(xf * xf, axis=-1, keepdims=True) + EPS)
    return (y * g.astype(jnp.float32)).astype(x.dtype)

def rope_tables(positions):
    inv_freq = ROPE_THETA ** (-jnp.arange(0, HEAD_DIM, 2, dtype=jnp.float32) / HEAD_DIM)
    ang = positions.astype(jnp.float32)[..., None] * inv_freq
    return jnp.cos(ang)[:, :, None, :], jnp.sin(ang)[:, :, None, :]

def apply_rope(x, cos, sin):
    xf = x.astype(jnp.float32)
    x1, x2 = xf[..., : HEAD_DIM // 2], xf[..., HEAD_DIM // 2:]
    out = jnp.concatenate([x1 * cos - x2 * sin, x2 * cos + x1 * sin], axis=-1)
    return out.astype(x.dtype)

def _lin_rec_combine(c1, c2):
    a1, b1 = c1
    a2, b2 = c2
    return a1 * a2, a2 * b1 + b2

def rglru_branch(u, gate, conv_w, conv_b, w_a, b_a, w_x, b_x, lam):
    B, S, _ = u.shape
    upad = jnp.pad(u, ((0, 0), (CONV_WIDTH - 1, 0), (0, 0)))
    uc = conv_b
    for k in range(CONV_WIDTH):
        uc = uc + upad[:, k:k + S] * conv_w[k]
    ub = uc.reshape(B, S, LRU_BLOCKS, LRU_BLOCK_DIM)
    r = jax.nn.sigmoid(jnp.einsum("bsnd,nde->bsne", ub, w_a) + b_a).reshape(B, S, LRU_WIDTH)
    i = jax.nn.sigmoid(jnp.einsum("bsnd,nde->bsne", ub, w_x) + b_x).reshape(B, S, LRU_WIDTH)
    log_a = -LRU_C * r.astype(jnp.float32) * jax.nn.softplus(-lam.astype(jnp.float32))
    a = jnp.exp(log_a)
    mult = jnp.sqrt(-jnp.expm1(2.0 * log_a))
    b = mult * i.astype(jnp.float32) * uc.astype(jnp.float32)
    _, h = lax.associative_scan(_lin_rec_combine, (a, b), axis=1)
    return (h * jax.nn.gelu(gate.astype(jnp.float32))).astype(u.dtype)

def _band(t, n_chunks):
    B, S, H, D = t.shape
    pad = (WINDOW_CHUNKS - 1) * CHUNK
    tp = jnp.pad(t, ((0, 0), (pad, 0), (0, 0), (0, 0)))
    tp = tp.reshape(B, n_chunks + WINDOW_CHUNKS - 1, CHUNK, H, D)
    return jnp.concatenate([tp[:, j:j + n_chunks] for j in range(WINDOW_CHUNKS)], axis=2)

def swa_sink_attention(q, k, v, cos, sin, sinks):
    B, S, _ = q.shape
    nC = S // CHUNK
    q = apply_rope(q.reshape(B, S, N_HEADS, HEAD_DIM), cos, sin)
    k = apply_rope(k.reshape(B, S, N_KV_HEADS, HEAD_DIM), cos, sin)
    v = v.reshape(B, S, N_KV_HEADS, HEAD_DIM)
    qc = q.reshape(B, nC, CHUNK, N_KV_HEADS, GROUP, HEAD_DIM)
    k_band = _band(k, nC)
    v_band = _band(v, nC)
    K = WINDOW_CHUNKS * CHUNK
    key_chunk = (jnp.arange(nC)[:, None] - (WINDOW_CHUNKS - 1)
                 + (jnp.arange(K) // CHUNK)[None, :])
    valid = (key_chunk >= 0)[:, None, :]
    s = jnp.einsum("bcqhgd,bckhd->bhgcqk", qc, k_band).astype(jnp.float32)
    s = jnp.where(valid, s * (1.0 / math.sqrt(HEAD_DIM)), NEG_INF)
    sink = jnp.broadcast_to(sinks.astype(jnp.float32).reshape(N_KV_HEADS, GROUP, 1, 1, 1),
                            s.shape[:-1] + (1,))
    p = jax.nn.softmax(jnp.concatenate([s, sink], axis=-1), axis=-1)[..., :-1]
    o = jnp.einsum("bhgcqk,bckhd->bcqhgd", p.astype(v.dtype), v_band)
    return o.reshape(B, S, ATTN_WIDTH)

def setup_inputs(seed: int = 0) -> dict:
    key = jax.random.key(seed)
    ks = jax.random.split(key, 24)
    f32 = jnp.float32

    def nrm(k, shape, fan_in):
        return jax.random.normal(k, shape, f32) * (fan_in ** -0.5)

    def gain(k):
        return 1.0 + 0.02 * jax.random.normal(k, (DEPTH, D_MODEL), f32)

    x = jax.random.normal(ks[0], (BATCH, SEQ, D_MODEL), f32)
    start = jax.random.randint(ks[1], (BATCH,), 0, 1024, dtype=jnp.int32) * CHUNK
    positions = start[:, None] + jnp.arange(SEQ, dtype=jnp.int32)[None, :]
    a0 = jax.random.uniform(ks[2], (DEPTH, LRU_WIDTH), f32, 0.9, 0.999)
    u0 = a0 ** (1.0 / LRU_C)
    lru_lambda = jnp.log(u0) - jnp.log1p(-u0)
    return {
        "x": x,
        "positions": positions,
        "pre_mix_g": gain(ks[3]),
        "w_in": nrm(ks[4], (DEPTH, D_MODEL, IN_WIDTH), D_MODEL),
        "conv_w": nrm(ks[5], (DEPTH, CONV_WIDTH, LRU_WIDTH), CONV_WIDTH),
        "conv_b": 0.01 * jax.random.normal(ks[6], (DEPTH, LRU_WIDTH), f32),
        "lru_wa": nrm(ks[7], (DEPTH, LRU_BLOCKS, LRU_BLOCK_DIM, LRU_BLOCK_DIM), LRU_BLOCK_DIM),
        "lru_ba": 0.01 * jax.random.normal(ks[8], (DEPTH, LRU_BLOCKS, LRU_BLOCK_DIM), f32),
        "lru_wx": nrm(ks[9], (DEPTH, LRU_BLOCKS, LRU_BLOCK_DIM, LRU_BLOCK_DIM), LRU_BLOCK_DIM),
        "lru_bx": 0.01 * jax.random.normal(ks[10], (DEPTH, LRU_BLOCKS, LRU_BLOCK_DIM), f32),
        "lru_lambda": lru_lambda,
        "attn_sinks": 0.5 * jax.random.normal(ks[11], (DEPTH, N_HEADS), f32),
        "w_pa": nrm(ks[12], (DEPTH, LRU_WIDTH, D_MODEL), LRU_WIDTH),
        "w_pb": nrm(ks[13], (DEPTH, ATTN_WIDTH, D_MODEL), ATTN_WIDTH),
        "w_o": nrm(ks[14], (DEPTH, D_MODEL, D_MODEL), D_MODEL),
        "post_mix_g": gain(ks[15]),
        "pre_ffn_g": gain(ks[16]),
        "w_ffn_gate": nrm(ks[17], (DEPTH, D_MODEL, D_FF), D_MODEL),
        "w_ffn_up": nrm(ks[18], (DEPTH, D_MODEL, D_FF), D_MODEL),
        "w_ffn_down": nrm(ks[19], (DEPTH, D_FF, D_MODEL), D_FF),
        "post_ffn_g": gain(ks[20]),
    }

def reference(x, positions, pre_mix_g, w_in, conv_w, conv_b, lru_wa, lru_ba, lru_wx, lru_bx,
              lru_lambda, attn_sinks, w_pa, w_pb, w_o, post_mix_g, pre_ffn_g,
              w_ffn_gate, w_ffn_up, w_ffn_down, post_ffn_g):
    cos, sin = rope_tables(positions)
    s1 = LRU_WIDTH
    s2 = s1 + LRU_WIDTH
    s3 = s2 + ATTN_WIDTH
    s4 = s3 + KV_WIDTH
    s5 = s4 + KV_WIDTH
    s6 = s5 + D_MODEL
    for l in range(DEPTH):
        xn = rmsnorm(x, pre_mix_g[l])
        proj = xn @ w_in[l]
        u_lru = proj[..., :s1]
        g_lru = proj[..., s1:s2]
        q = proj[..., s2:s3]
        k = proj[..., s3:s4]
        v = proj[..., s4:s5]
        gate_a = jax.nn.sigmoid(proj[..., s5:s6])
        gate_b = jax.nn.sigmoid(proj[..., s6:])
        y_a = rglru_branch(u_lru, g_lru, conv_w[l], conv_b[l], lru_wa[l], lru_ba[l],
                           lru_wx[l], lru_bx[l], lru_lambda[l]) @ w_pa[l]
        y_b = swa_sink_attention(q, k, v, cos, sin, attn_sinks[l]) @ w_pb[l]
        mixed = (gate_a * y_a + gate_b * y_b) @ w_o[l]
        x = x + rmsnorm(mixed, post_mix_g[l])
        h = rmsnorm(x, pre_ffn_g[l])
        f = (jax.nn.silu(h @ w_ffn_gate[l]) * (h @ w_ffn_up[l])) @ w_ffn_down[l]
        x = x + rmsnorm(f, post_ffn_g[l])
    return x


_drawn_inputs = setup_inputs


def setup_inputs(seed=0):
    import zlib

    import numpy as np

    out = dict(_drawn_inputs(seed))
    spreads = {}
    factors = {'lru_ba': 23.346, 'lru_bx': 8.0, 'attn_sinks': 8.0, 'post_ffn_g': 3.559}
    for name, (base, spread) in spreads.items():
        noise = np.random.default_rng([zlib.crc32(name.encode()), seed]).standard_normal(out[name].shape)
        drawn = base * np.exp(spread * noise) if base else spread * noise
        out[name] = __import__('jax').numpy.asarray(drawn.astype(out[name].dtype))
    for name, factor in factors.items():
        out[name] = (out[name] * factor).astype(out[name].dtype)
    return out
```

```python
from contextlib import ExitStack

import numpy as np

import concourse.bass as bass
from concourse import mybir

P = 128
F32 = mybir.dt.float32
F32R = mybir.dt.float32r
I32 = mybir.dt.int32
ALU = mybir.AluOpType
ACT = mybir.ActivationFunctionType
AX = mybir.AxisListType

HEAD_DIM = 64
CHUNK = 64
ROPE_THETA = 10000.0
LRU_C = 8.0
EPS = 1e-6
GELU_CUBE = 0.044715
GELU_SCALE = 0.7978845608028654

RAW = 2
RING = 4
PANEL = 2048


class Signal:

    def __init__(self, sem, per_layer, start=0):
        self.sem, self.per_layer, self.start = sem, per_layer, start

    def at(self, layer, n):
        assert 1 <= n <= self.per_layer
        return self.sem, layer * self.per_layer + (self.start + n)


def panel_plan(n_pairs):
    plan = [("u", j) for j in range(4)]
    plan += [("kv", 0), ("kv", 1), ("q0", 0), ("q0", 1), ("q1", 0), ("q1", 1)]
    for name in ("gelu", "gate_a", "gate_b", "pa", "pb", "wo"):
        plan += [(name, j) for j in range(4)]
    tail = 3
    for j in range(n_pairs):
        plan += [("ffn_gate", j), ("ffn_up", j)]
        if 1 <= j <= n_pairs - tail:
            plan.append(("down", j - 1))
    plan += [("down", j) for j in range(n_pairs - tail, n_pairs)]
    return plan, tail


def trunk(nc, x, positions, pre_mix_g, w_in, conv_w, conv_b, lru_wa, lru_ba, lru_wx, lru_bx,
          lru_lambda, attn_sinks, w_pa, w_pb, w_o, post_mix_g, pre_ffn_g, w_ffn_gate, w_ffn_up,
          w_ffn_down, post_ffn_g, out):
    _, S, D = x.shape
    DEPTH = w_in.shape[0]
    NT = S // P
    KD = D // P
    NP = w_ffn_gate.shape[2] // 256
    NH = attn_sinks.shape[1]
    NC = S // CHUNK
    CW = conv_w.shape[1]
    assert (S, D, NT, KD, NH, NC, CW) == (256, 1024, 2, 8, 16, 4, 4)
    PLAN, TAIL = panel_plan(NP)
    NPAN = len(PLAN)
    AT = {name: n for n, name in enumerate(PLAN)}
    COL_U, COL_G, COL_Q, COL_KV, COL_GA, COL_GB = 0, 1024, 2048, 3072, 3584, 4608

    with ExitStack() as ctx:
        def sb(name, shape, dt=F32):
            return ctx.enter_context(nc.sbuf_tensor(name, shape, dt))

        def sem(name):
            return ctx.enter_context(nc.semaphore(name))

        def signal(name, per_layer, start=0):
            return Signal(sem(name), per_layer, start)

        raw = sb("weights_raw", [P, RAW, PANEL])
        w_hi = sb("weights_hi", [P, RING, PANEL], F32R)
        w_lo = sb("weights_lo", [P, RING, PANEL], F32R)
        XA = [sb(f"act_a_{s}", [P, KD, S], F32R) for s in ("hi", "lo")]
        XB = [sb(f"act_b_{s}", [P, KD, S], F32R) for s in ("hi", "lo")]
        xres = sb("x_residual", [P, NT, D])
        g_pre = sb("gain_pre", [P, D])
        g_post = sb("gain_post", [P, D])
        bd_a = sb("blockdiag_wa", [P, KD, P])
        bd_x = sb("blockdiag_wx", [P, KD, P])
        U = sb("lru_u", [P, KD, S + CW - 1])
        UC = sb("lru_uc", [P, KD, S])
        IG = sb("lru_i", [P, KD, S])
        AG = sb("lru_a", [P, KD, S])
        QTOK = sb("q_tok", [P, NT, D])
        KTOK = sb("k_tok", [P, NT, 4, P])
        VT = sb("v_tok", [P, NT, 256])
        VS = sb("v_shifted", [P, 256])
        QT = sb("q_feat", [P, KD, S])
        KT = sb("k_feat", [P, 4, S])
        GT = sb("temps", [P, 2, 512])
        ident = sb("identity", [P, P])
        vec_rows = sb("vector_rows", [DEPTH * 8 * KD, P])
        vecs = sb("vectors", [P, DEPTH, 10, KD])
        vec = sb("vectors_of_layer", [P, 10, KD])
        sink_rows = sb("sink_rows", [P, DEPTH, NH])
        sinks = sb("sinks", [P, DEPTH, 8])
        sink = sb("sinks_of_layer", [P, 8])
        pos_i = sb("pos_int", [P, NT], I32)
        pos_f = sb("pos_float", [P, NT])
        inv_freq = sb("inv_freq", [P, 32])
        ang = sb("angle", [P, NT, 32])
        digit = [sb(f"turns_{n}", [P, NT, 32]) for n in range(3)]
        cos = sb("cos", [P, NT, 32])
        sin = sb("sin_signed", [P, NT, 2, 32])
        sp_t = sb("softplus_t", [P, DEPTH, KD])
        sp_s = sb("softplus_s", [P, DEPTH, KD])
        sp_p = sb("softplus_p", [P, DEPTH, KD])
        mean_sq = sb("mean_square", [P, 8])
        ms_eps = sb("mean_square_eps", [P, 8])
        rstd = sb("rstd", [P, 8])
        eps_t = sb("eps", [P, 1])
        mhalf = sb("minus_half", [P, 1])
        sm = sb("softmax_small", [P, 8, 8, 4])

        def bits(ap):
            return ap.bitcast(F32)

        def f_panel(ring, slot):
            return ring[:, slot, :].rearrange("p (k f) -> p k f", k=KD)

        def t_panel(ring, slot, kc):
            return ring[:, slot, :].rearrange("p (k f) -> p k f", k=kc)

        xn_hi, xn_lo = XA
        z_hi, z_lo = XB
        thA, thB = QTOK[:, :, :].rearrange("p t (k s) -> p (t k) s", s=S), AG
        junk = KTOK[:, :, :, :].rearrange("p t g d -> p (t g d)")
        h_lru = U[:, :, CW - 1:]
        f_th_t = IG[:, 0:4, :].rearrange("p (b k) s -> p b (k s)", b=2)
        f_silu_t = IG[:, 4:8, :].rearrange("p (b k) s -> p b (k s)", b=2)
        f_prod_t = AG[:, 0:4, :].rearrange("p (b k) s -> p b (k s)", b=2)

        q_rows = QT[:, :, :].rearrange("p (c a) s -> p c (a s)", c=NC)

        def prob(c, par):
            k = 4 * (c % 2) + 2 * par
            return U[:, k:k + 2, CW - 1:].rearrange("p r (h k) -> p r h k", h=2)

        def prob_t(c):
            return UC[:, 4 * (c % 2):4 * (c % 2) + 4, :].rearrange("p a (h k) -> p (a h) k", h=2)

        def key_span(c):
            return (0, CHUNK) if c == 0 else (CHUNK * (c - 1), 2 * CHUNK)

        work = [ctx.enter_context(nc.psum_tensor(f"work_{b}", [P, 512], F32)) for b in range(4)]
        acc = ctx.enter_context(nc.psum_tensor("acc", [P, 4, 512], F32))

        raw_loaded = [signal(f"raw_loaded_{s}", (NPAN + RAW - 1 - s) // RAW * 16) for s in range(RAW)]
        hi_done = signal("panel_hi_done", NPAN)
        split_done = signal("panel_split_done", NPAN, 1)
        panel_used = signal("panel_used", NPAN)
        bd_loaded = signal("blockdiag_loaded", 64)
        pre_loaded = signal("gain_pre_loaded", 32)
        post_loaded = signal("gain_post_loaded", 32)
        ms_done = signal("mean_square_done", 8)
        rstd_done = signal("rstd_done", 8)
        xs_done = signal("normed_tile_done", 4)
        turned = signal("x_turned", 8)
        xa_hi_done = signal("xa_hi_done", 8)
        xa_done = signal("xa_done", 8)
        u_done = signal("u_copied", 4)
        uc_done = signal("conv_done", 8)
        gates_mm = signal("gates_multiplied", 8)
        gates_done = signal("gate_sigmoids_done", 8)
        a_done = signal("decay_done", 2)
        v_done = signal("mult_square_done", 2)
        mult_done = signal("mult_done", 2)
        h_done = signal("scan_done", 2)
        roped = signal("rope_done", 6)
        rope_read = signal("rope_psum_read", 6)
        qk_turned = signal("qk_turned", 6)
        qk_done = signal("qk_feat_done", 6)
        g_sq = signal("gelu_square", 4)
        g_in = signal("gelu_inner", 4)
        g_th = signal("gelu_tanh", 4)
        g_read = signal("gelu_psum_read", 4)
        z_done = signal("z_done", 4)
        z_hi_done = signal("z_hi_done", 4)
        z_lo_done = signal("z_lo_done", 4)
        gate_th = signal("merge_gate_tanh", 8)
        scored = signal("scores_multiplied", 8)
        bias_done = signal("softmax_bias_done", 8)
        score_read = signal("scores_read", 8)
        sink_exp = signal("sink_exp_done", 8)
        p_done = signal("p_done", 8)
        p_turned = signal("p_turned", 8)
        pt_done = signal("p_feat_done", 8)
        pv = signal("pv_multiplied", 4)
        o_hi_done = signal("o_hi_done", 4)
        o_done = signal("o_done", 4)
        ya_read = signal("ya_read", 4)
        yb_read = signal("yb_read", 4)
        m_done = signal("mixed_done", 4)
        m_hi_done = signal("mixed_hi_done", 4)
        m_lo_done = signal("mixed_lo_done", 4)
        tile0 = signal("first_tile_multiplied", 2)
        branch_read = signal("branch_psum_read", 4)
        x_done = signal("x_updated", 4, 1)
        f_th = signal("silu_tanh", NP)
        f_gate = signal("silu_done", NP)
        f_up = signal("ffn_product_done", NP)
        f_hi_done = signal("ffn_hi_done", NP)
        f_done = signal("ffn_done", NP)
        x_loaded, rows_loaded, pos_loaded, sinks_loaded = (
            sem(n) for n in ("x_loaded", "rows_loaded", "pos_loaded", "sinks_loaded"))
        cleared, ident_done, consts_done = (sem(n) for n in ("cleared", "ident_done", "consts_done"))
        vec_turned, sines_ready, sines_done, exp_ready, exp_done, setup_done = (
            sem(n) for n in ("vec_turned", "sines_ready", "sines_done", "exp_ready", "exp_done", "setup_done"))
        dve_step, act_step, pool_step, stored = (
            sem(n) for n in ("dve_step", "act_step", "pool_step", "stored"))

        USES = [("xn", n) for n in range(4)] + [("u", n) for n in range(4)]
        USES += [("gates", n) for n in range(8)] + [("turn", n) for n in range(6)]
        USES += [("gelu", n) for n in range(4)] + [("gate_a", n) for n in range(4)]
        USES += [("gate_b", n) for n in range(4)] + [("pv", 0), ("pv", 1), ("pa", 0), ("pa", 1)]
        USES += [("pv", 2), ("pa", 2), ("pv", 3), ("pa", 3)] + [("pb", n) for n in range(4)]
        USES += [("h", n) for n in range(4)]
        for j in range(NP):
            USES += [("ffn_gate", j), ("ffn_up", j)]
        USE = {name: n for n, name in enumerate(USES)}
        FREED_BY = {"xn": (xa_done, 0), "u": (u_done, 0), "gates": (gates_done, 0), "turn": (qk_done, 0),
                    "gelu": (g_read, 0), "gate_a": (gate_th, 0), "gate_b": (gate_th, 4),
                    "pv": (o_done, 0), "pa": (ya_read, 0), "pb": (yb_read, 0), "h": (xa_done, 4),
                    "ffn_gate": (f_gate, 0), "ffn_up": (f_up, 0)}

        def bank(name, n):
            return work[USE[name, n] % 4]

        block = ctx.enter_context(nc.Block())

        @block.sync
        def _(sp):
            sp.dma_start(xres[:, 0, :], x[0, 0:P, :]).then_inc(x_loaded, 16)
            sp.dma_start(xres[:, 1, :], x[0, P:S, :]).then_inc(x_loaded, 16)
            for l in range(DEPTH):
                for v, src in enumerate((conv_w, conv_b, lru_ba, lru_bx, lru_lambda)):
                    row = (l * 8 + (0 if v == 0 else CW + v - 1)) * KD
                    if v == 0:
                        part, n = src[l].rearrange("c (k p) -> (c k) p", p=P), CW * KD
                    elif v in (2, 3):
                        part, n = src[l].rearrange("(k b) e -> k (b e)", b=2), KD
                    else:
                        part, n = src[l].rearrange("(k p) -> k p", p=P), KD
                    sp.dma_start(vec_rows[row:row + n, :], part).then_inc(rows_loaded, 16)
            sp.dma_start(pos_i[:, :], positions.rearrange("a (t p) -> p (a t)", p=P),
                         allow_slow_non_contiguous=True).then_inc(pos_loaded, 16)
            sp.dma_start(sink_rows[:, :, :], attn_sinks.rearrange("l h -> (l h)").partition_broadcast(P)
                         .rearrange("p (l h) -> p l h", l=DEPTH)).then_inc(sinks_loaded, 16)
            sp.sem_inc(split_done.sem, 1)
            sp.wait_ge(cleared, 2)
            with sp.Fori(0, DEPTH) as l:
                for n, (name, j) in enumerate(PLAN):
                    if n < RAW:
                        sp.wait_ge(split_done.sem, l * NPAN + 1)
                    else:
                        sp.wait_ge(*split_done.at(l, n - RAW + 1))
                    if n == 0:
                        sp.dma_start(g_pre[:, :], pre_mix_g[l].partition_broadcast(P)).then_inc(pre_loaded.sem, 16)
                    if name in ("u", "gelu", "gate_a", "gate_b"):
                        c = {"u": COL_U, "gelu": COL_G, "gate_a": COL_GA, "gate_b": COL_GB}[name] + 256 * j
                        src = w_in[l][:, c:c + 256]
                    elif name in ("kv", "q0", "q1"):
                        c = {"kv": COL_KV, "q0": COL_Q, "q1": COL_Q + 512}[name]
                        src = w_in[l][512 * j:512 * j + 512, c:c + 512]
                    elif name in ("pa", "pb", "ffn_gate", "ffn_up"):
                        w = {"pa": w_pa, "pb": w_pb, "ffn_gate": w_ffn_gate, "ffn_up": w_ffn_up}[name]
                        src = w[l][:, 256 * j:256 * j + 256]
                    else:
                        src = (w_o if name == "wo" else w_ffn_down)[l][256 * j:256 * j + 256, :]
                    kc = src.shape[0] // P
                    sp.dma_start(t_panel(raw, n % RAW, kc), src.rearrange("(k p) f -> p k f", p=P)
                                 ).then_inc(raw_loaded[n % RAW].sem, 16)
                    if n == 4:
                        for b in range(2):
                            for dst, src in ((bd_a, lru_wa), (bd_x, lru_wx)):
                                sp.dma_start(dst[64 * b:64 * b + 64, :, 64 * b:64 * b + 64],
                                             src[l].rearrange("(k b) d e -> b d k e", b=2)[b]
                                             ).then_inc(bd_loaded.sem, 16)
                        sp.dma_start(g_post[:, :], post_mix_g[l].partition_broadcast(P)).then_inc(post_loaded.sem, 16)
                    if n == AT["gelu", 0]:
                        sp.dma_start(g_pre[:, :], pre_ffn_g[l].partition_broadcast(P)).then_inc(pre_loaded.sem, 16)
                    if n == AT["down", 0] + RAW + RING:
                        sp.dma_start(g_post[:, :], post_ffn_g[l].partition_broadcast(P)).then_inc(post_loaded.sem, 16)
            for t in range(NT):
                sp.wait_ge(*x_done.at(DEPTH - 1, 3 + t))
                sp.dma_start(out[0, P * t:P * t + P, :], xres[:, t, :]).then_inc(stored, 16)
            sp.wait_ge(stored, 32)

        @block.gpsimd
        def _(pool):
            nc.gpsimd.memset(ident[:, :], 0.0).then_inc(pool_step, 1)
            nc.gpsimd.memset(bd_a[:, :, :], 0.0).then_inc(cleared, 1)
            nc.gpsimd.memset(bd_x[:, :, :], 0.0).then_inc(cleared, 1)
            pool.wait_ge(pool_step, 1)
            nc.gpsimd.affine_select(out=ident[:, :], in_=ident[:, :], compare_op=ALU.not_equal, fill=1.0,
                                    base=0, pattern=[[-1, P]], channel_multiplier=1).then_inc(ident_done, 1)
            nc.gpsimd.memset(eps_t[:, :], EPS).then_inc(pool_step, 1)
            nc.gpsimd.memset(mhalf[:, :], -0.5).then_inc(pool_step, 1)
            nc.gpsimd.memset(U[:, :, 0:CW - 1], 0.0).then_inc(pool_step, 1)
            freq = ROPE_THETA ** (-np.arange(0, HEAD_DIM, 2) / HEAD_DIM)
            for i, v in enumerate(freq.astype(np.float32)):
                ins = nc.gpsimd.memset(inv_freq[:, i:i + 1], float(v))
            ins.then_inc(consts_done, 1)
            pool.wait_ge(pool_step, 4)
            with pool.Fori(0, DEPTH) as l:
                for n in range(8):
                    pool.wait_ge(*ms_done.at(l, n + 1))
                    nc.gpsimd.tensor_tensor(ms_eps[:, n:n + 1], mean_sq[:, n:n + 1], eps_t[:, :],
                                            ALU.add).then_inc(pool_step, 1)
                    pool.wait_ge(pool_step, l * 8 + (5 + n))
                    nc.gpsimd.tensor_tensor(rstd[:, n:n + 1], ms_eps[:, n:n + 1], mhalf[:, :],
                                            ALU.pow).then_inc(rstd_done.sem, 1)

        @block.tensor
        def _(pe):
            mm = nc.tensor.matmul

            pe.wait_ge(ident_done, 1)
            pe.wait_ge(rows_loaded, 16 * 5 * DEPTH)
            nc.tensor.transpose(work[0][:, 0:P], vec_rows[:, :], ident[:, :]).then_inc(vec_turned, 1)
            pe.wait_ge(setup_done, 1)

            with pe.Fori(0, DEPTH) as l:
                def claim(name, n):
                    k = USE[name, n]
                    if k >= 4:
                        before, m = USES[k - 4]
                        freed, first = FREED_BY[before]
                        pe.wait_ge(*freed.at(l, first + m + 1))
                    return work[k % 4]

                def turn_x(first, name, t):
                    for h in range(2):
                        dst = claim(name, 2 * t + h)
                        if h == 0:
                            pe.wait_ge(*xs_done.at(l, first // 2 + t + 1))
                        for k in range(4):
                            f = (4 * h + k) * P
                            last = nc.tensor.transpose(dst[:, k * P:k * P + P], QTOK[:, t, f:f + P], ident[:, :])
                        last.then_inc(turned.sem, 1)

                def split_ready(n):
                    pe.wait_ge(*split_done.at(l, n + 1))

                def f_product(name, j, hi, lo):
                    n = AT[name, j]
                    dst = claim(name, j)
                    split_ready(n)
                    wh, wl = f_panel(w_hi, n % RING), f_panel(w_lo, n % RING)
                    for c in range(2):
                        o = dst[:, c * S:c * S + S]
                        for k in range(KD):
                            h, w = wh[:, k, c * P:c * P + P], wl[:, k, c * P:c * P + P]
                            mm(o, h, hi[:, k, :], start=k == 0, stop=False)
                            mm(o, h, lo[:, k, :], start=False, stop=False)
                            last = mm(o, w, hi[:, k, :], start=False, stop=k == KD - 1)
                    last.then_inc(panel_used.sem, 1)

                def t_products(dst, hi, lo, k, t, wh, wl, first, final):
                    xh, xl = hi[:, k, t * P:t * P + P], lo[:, k, t * P:t * P + P]
                    mm(dst, xh, wh, start=first, stop=False)
                    mm(dst, xh, wl, start=False, stop=False)
                    return mm(dst, xl, wh, start=False, stop=final)

                def qkv_product(name, b):
                    for j in range(2):
                        n = AT[name, j]
                        split_ready(n)
                        wh, wl = t_panel(w_hi, n % RING, 4), t_panel(w_lo, n % RING, 4)
                        for t in range(NT):
                            for k in range(4):
                                last = t_products(acc[:, b + t, :], xn_hi, xn_lo, 4 * j + k, t,
                                                  wh[:, k, :], wl[:, k, :], j == 0 and k == 0, j == 1 and k == 3)
                        last.then_inc(panel_used.sem, 1)

                def row_panel(n, k0, hi, lo, t, first, final):
                    wh, wl = t_panel(w_hi, n % RING, 2), t_panel(w_lo, n % RING, 2)
                    for kk in range(2):
                        for half in range(2):
                            cols = slice(512 * half, 512 * half + 512)
                            last = t_products(acc[:, 2 * t + half, :], hi, lo, k0 + kk, t, wh[:, kk, cols],
                                              wl[:, kk, cols], first and kk == 0, final and kk == 1)
                    return last

                def scores(c):
                    k0, nk = key_span(c)
                    for par in range(2):
                        if c == 0:
                            pe.wait_ge(*rope_read.at(l, 5 + par))
                        else:
                            pe.wait_ge(*score_read.at(l, 2 * c - 1 + par))
                        rows = slice(64 * par, 64 * par + 64)
                        for g in range(4):
                            last = mm(acc[:, par, g * P:g * P + nk],
                                      q_rows[rows, c, 2 * g * CHUNK:2 * (g + 1) * CHUNK],
                                      KT[rows, g, k0:k0 + nk], start=True, stop=True)
                        last.then_inc(scored.sem, 1)

                def turn_p(c):
                    for par in range(2):
                        if c == 0:
                            pe.wait_ge(*rope_read.at(l, 3 + par))
                        else:
                            pe.wait_ge(*pt_done.at(l, 2 * c - 1 + par))
                        pe.wait_ge(*p_done.at(l, 2 * c + par + 1))
                        for g in range(4):
                            last = nc.tensor.transpose(acc[:, 2 + par, g * P:g * P + P],
                                                       prob(c, par)[:, g // 2, g % 2, :], ident[:, :])
                        last.then_inc(p_turned.sem, 1)

                def pv_product(c):
                    dst = claim("pv", c)
                    pe.wait_ge(*pt_done.at(l, 2 * c + 2))
                    v = VT[:, c // 2, :] if c in (0, 1, 3) else VS[:, :]
                    for par in range(2):
                        for g in range(4):
                            last = mm(dst[64 * par:64 * par + 64, g * P:g * P + P], v[:, 64 * g:64 * g + 64],
                                      prob_t(c)[:, 4 * par + g, :], start=True, stop=True)
                    last.then_inc(pv.sem, 1)

                turn_x(0, "xn", 0)
                turn_x(0, "xn", 1)
                pe.wait_ge(*xa_done.at(l, 4))
                for j in range(4):
                    f_product("u", j, xn_hi, xn_lo)
                qkv_product("kv", 0)
                qkv_product("q0", 2)
                for t in range(NT):
                    pe.wait_ge(*rope_read.at(l, 1 + t))
                qkv_product("q1", 0)
                pe.wait_ge(*bd_loaded.at(l, 64))
                for c in range(KD):
                    dst = claim("gates", c)
                    pe.wait_ge(*uc_done.at(l, c + 1))
                    mm(dst[:, 0:S], bd_a[:, c, :], UC[:, c, :], start=True, stop=True)
                    mm(dst[:, S:2 * S], bd_x[:, c, :], UC[:, c, :], start=True, stop=True).then_inc(gates_mm.sem, 1)
                for n in range(6):
                    dst = claim("turn", n)
                    pe.wait_ge(*roped.at(l, 6))
                    for k in range(4):
                        if n < 4:
                            t, h = n // 2, n % 2
                            src = QTOK[:, t, (4 * h + k) * P:(4 * h + k + 1) * P]
                        else:
                            src = KTOK[:, n - 4, k, :]
                        last = nc.tensor.transpose(dst[:, k * P:k * P + P], src, ident[:, :])
                    last.then_inc(qk_turned.sem, 1)
                for j in range(4):
                    f_product("gelu", j, xn_hi, xn_lo)
                f_product("gate_a", 0, xn_hi, xn_lo)
                f_product("gate_a", 1, xn_hi, xn_lo)
                pe.wait_ge(*qk_done.at(l, 6))
                scores(0)
                f_product("gate_a", 2, xn_hi, xn_lo)
                f_product("gate_a", 3, xn_hi, xn_lo)
                turn_p(0)
                scores(1)
                f_product("gate_b", 0, xn_hi, xn_lo)
                f_product("gate_b", 1, xn_hi, xn_lo)
                turn_p(1)
                scores(2)
                f_product("gate_b", 2, xn_hi, xn_lo)
                f_product("gate_b", 3, xn_hi, xn_lo)
                pv_product(0)
                pv_product(1)
                turn_p(2)
                scores(3)
                pe.wait_ge(*z_lo_done.at(l, 4))
                f_product("pa", 0, z_hi, z_lo)
                f_product("pa", 1, z_hi, z_lo)
                pv_product(2)
                turn_p(3)
                f_product("pa", 2, z_hi, z_lo)
                pv_product(3)
                f_product("pa", 3, z_hi, z_lo)
                pe.wait_ge(*o_done.at(l, 4))
                for j in range(4):
                    f_product("pb", j, xn_hi, xn_lo)
                pe.wait_ge(*m_lo_done.at(l, 4))
                for t in range(NT):
                    for j in range(4):
                        n = AT["wo", j]
                        if t == 0:
                            split_ready(n)
                            if j == 0:
                                pe.wait_ge(*score_read.at(l, 8))
                                pe.wait_ge(*pt_done.at(l, 8))
                        last = row_panel(n, 2 * j, z_hi, z_lo, t, j == 0, j == 3)
                        if t == NT - 1:
                            last.then_inc(panel_used.sem, 1)
                        elif j == 3:
                            last.then_inc(tile0.sem, 1)
                turn_x(4, "h", 0)
                turn_x(4, "h", 1)
                pe.wait_ge(*xa_done.at(l, 8))
                for name, j in PLAN[AT["ffn_gate", 0]:AT["down", NP - TAIL]]:
                    if name != "down":
                        f_product(name, j, xn_hi, xn_lo)
                        continue
                    n = AT[name, j]
                    split_ready(n)
                    pe.wait_ge(*f_done.at(l, j + 1))
                    if j == 0:
                        pe.wait_ge(*branch_read.at(l, 2))
                    for t in range(NT):
                        last = row_panel(n, 2 * (j % 4), z_hi, z_lo, t, j == 0, False)
                    last.then_inc(panel_used.sem, 1)
                for t in range(NT):
                    for j in range(NP - TAIL, NP):
                        n = AT["down", j]
                        if t == 0:
                            split_ready(n)
                            pe.wait_ge(*f_done.at(l, j + 1))
                        last = row_panel(n, 2 * (j % 4), z_hi, z_lo, t, False, j == NP - 1)
                        if t == NT - 1:
                            last.then_inc(panel_used.sem, 1)
                        elif j == NP - 1:
                            last.then_inc(tile0.sem, 1)

        @block.scalar
        def _(act):
            step = [0]

            def own(ins):
                step[0] += 1
                ins.then_inc(act_step, 1)
                act.wait_ge(act_step, step[0])

            activate = nc.scalar.activation

            act.wait_ge(sines_ready, 1)
            own(activate(sin[:, :, 0, :], ang[:, :, :], ACT.Sin, scale=-1.0))
            own(activate(sin[:, :, 1, :], ang[:, :, :], ACT.Sin))
            activate(cos[:, :, :], digit[0][:, :, :], ACT.Sin).then_inc(sines_done, 1)
            act.wait_ge(exp_ready, 1)
            activate(sp_t[:, :, :], sp_s[:, :, :], ACT.Exp, scale=-1.0).then_inc(exp_done, 1)
            act.wait_ge(setup_done, 1)
            act.wait_ge(x_loaded, 32)
            act.sem_inc(x_done.sem, 1)
            own(activate(junk[:, 0:1], eps_t[:, :], ACT.Copy))
            act.sem_clear(act_step)
            step[0] = 0

            with act.Fori(0, DEPTH) as l:
                def done(ins, sig, n):
                    ins.then_inc(sig.sem, 1)
                    act.wait_ge(*sig.at(l, n))

                def split_hi(n):
                    if n >= NPAN:
                        return
                    act.wait_ge(*raw_loaded[n % RAW].at(l, 16 * (n // RAW + 1)))
                    if n >= RING:
                        act.wait_ge(*panel_used.at(l, n - RING + 1))
                    activate(w_hi[:, n % RING, :], raw[:, n % RAW, :], ACT.Copy).then_inc(hi_done.sem, 1)

                def mean_square(n, src):
                    done(activate(junk[:, :], src, ACT.Square, scale=D ** -0.5,
                                  accum_out=mean_sq[:, n:n + 1]), ms_done, n + 1)

                def xa_hi(first, name, t, h):
                    act.wait_ge(*turned.at(l, first + 2 * t + h + 1))
                    done(activate(xn_hi[:, 4 * h:4 * h + 4, P * t:P * t + P],
                                  bank(name, 2 * t + h)[:, :].rearrange("p (k s) -> p k s", k=4), ACT.Copy),
                         xa_hi_done, first + 2 * t + h + 1)

                def used(name, j):
                    act.wait_ge(*panel_used.at(l, AT[name, j] + 1))
                    return bank(name, j)[:, :]

                def two(t, j):
                    return t[:, 2 * j:2 * j + 2, :]

                def pair(ps):
                    return ps.rearrange("p (k s) -> p k s", k=2)

                def decay(half):
                    for c in range(4 * half, 4 * half + 4):
                        own(activate(AG[:, c, :], h_lru[:, c, :], ACT.Exp, scale=vec[:, 8, c:c + 1]))
                        ins = activate(h_lru[:, c, :], h_lru[:, c, :], ACT.Tanh, scale=vec[:, 9, c:c + 1])
                        if c % 4 < 3:
                            own(ins)
                    done(ins, a_done, half + 1)

                def gelu_square(j):
                    if j >= 2:
                        act.wait_ge(*z_lo_done.at(l, j - 1))
                    done(activate(GT[:, j % 2, :], used("gelu", j), ACT.Square), g_sq, j + 1)

                def gelu_tanh(j):
                    act.wait_ge(*g_in.at(l, j + 1))
                    done(activate(GT[:, j % 2, :], GT[:, j % 2, :], ACT.Tanh, scale=GELU_SCALE), g_th, j + 1)

                def z_hi_part(j):
                    act.wait_ge(*z_done.at(l, j + 1))
                    done(activate(two(z_hi, j), pair(GT[:, j % 2, :]), ACT.Copy), z_hi_done, j + 1)

                def gate(name, dst, j):
                    n = j + (0 if name == "gate_a" else 4)
                    done(activate(dst[:, 2 * j:2 * j + 2, :], pair(used(name, j)), ACT.Tanh, scale=0.5),
                         gate_th, n + 1)

                def exps(c):
                    _, nk = key_span(c)
                    for par in range(2):
                        u = 2 * c + par
                        act.wait_ge(*bias_done.at(l, u + 1))
                        for g in range(4):
                            ins = activate(prob(c, par)[:, g // 2, g % 2, 0:nk], acc[:, par, g * P:g * P + nk],
                                           ACT.Exp, bias=sm[:, u, 2, g:g + 1], scale=HEAD_DIM ** -0.5,
                                           accum_out=sm[:, u, 3, g:g + 1])
                            if g < 3:
                                own(ins)
                        done(ins, score_read, u + 1)
                        done(activate(sm[:, u, 5, :], sm[:, u, 4, :], ACT.Exp), sink_exp, u + 1)

                def p_copy(c):
                    for par in range(2):
                        act.wait_ge(*p_turned.at(l, 2 * c + par + 1))
                        done(activate(prob_t(c)[:, 4 * par:4 * par + 4, :],
                                      acc[:, 2 + par, :].rearrange("p (g s) -> p g s", g=4), ACT.Copy),
                             pt_done, 2 * c + par + 1)

                def o_hi_part(c):
                    act.wait_ge(*pv.at(l, c + 1))
                    done(activate(xn_hi[:, :, CHUNK * c:CHUNK * c + CHUNK],
                                  bank("pv", c)[:, :].rearrange("p (k s) -> p k s", k=KD), ACT.Copy),
                         o_hi_done, c + 1)

                act.wait_ge(x_done.sem, l * 4 + 1)
                for t in range(NT):
                    mean_square(t, xres[:, t, :])
                split_hi(0)
                for t in range(NT):
                    for h in range(2):
                        xa_hi(0, "xn", t, h)
                for n in range(1, RING):
                    split_hi(n)

                for n, (name, j) in enumerate(PLAN):
                    if name == "u":
                        done(activate(two(U[:, :, CW - 1:], j), pair(used("u", j)), ACT.Copy), u_done, j + 1)
                    if (name, j) == ("q1", 1):
                        for c in range(KD):
                            act.wait_ge(*gates_mm.at(l, c + 1))
                            ps = bank("gates", c)
                            own(activate(h_lru[:, c, :], ps[:, 0:S], ACT.Sigmoid, bias=vec[:, 5, c:c + 1]))
                            done(activate(IG[:, c, :], ps[:, S:2 * S], ACT.Sigmoid, bias=vec[:, 6, c:c + 1]),
                                 gates_done, c + 1)
                        for m in range(6):
                            act.wait_ge(*qk_turned.at(l, m + 1))
                            ps, t, h = bank("turn", m)[:, :], m // 2, m % 2
                            if m < 4:
                                src = ps.rearrange("p (k c s) -> p k c s", k=4, c=2)
                                dst = q_rows[:, 2 * t:2 * t + 2, :].rearrange(
                                    "p c (k s) -> p k c s", s=CHUNK)[:, 4 * h:4 * h + 4, :, :]
                            else:
                                src = ps.rearrange("p (k s) -> p k s", k=4)
                                dst = KT[:, :, P * (m - 4):P * (m - 3)]
                            done(activate(dst, src, ACT.Copy), qk_done, m + 1)
                    if name == "gelu":
                        if j >= 2:
                            z_hi_part(j - 2)
                        gelu_square(j)
                        if j < 2:
                            decay(j)
                        gelu_tanh(j)
                        if j == 1:
                            for half in range(2):
                                act.wait_ge(*v_done.at(l, half + 1))
                                v = UC[:, 4 * half:4 * half + 4, :]
                                done(activate(v, v, ACT.Sqrt), mult_done, half + 1)
                    if (name, j) == ("gate_a", 0):
                        z_hi_part(2)
                        z_hi_part(3)
                    if name == "gate_a":
                        gate("gate_a", thA, j)
                    if name == "gate_b":
                        if j == 0:
                            act.wait_ge(*h_done.at(l, 2))
                        gate("gate_b", thB, j)
                    if (name, j) == ("pb", 3):
                        act.wait_ge(*m_done.at(l, j + 1))
                        done(activate(two(z_hi, j), two(IG, j), ACT.Copy, scale=0.5), m_hi_done, j + 1)
                    if (name, j) == ("wo", 0):
                        act.wait_ge(*tile0.at(l, 1))
                        mean_square(2, acc[:, 0:2, :].rearrange("p b f -> p (b f)"))
                        act.wait_ge(*x_done.at(l, 1))
                        mean_square(3, xres[:, 0, :])
                    if (name, j) == ("wo", 3):
                        act.wait_ge(*panel_used.at(l, n + 1))
                        mean_square(4, acc[:, 2:4, :].rearrange("p b f -> p (b f)"))
                        xa_hi(4, "h", 0, 0)
                        xa_hi(4, "h", 0, 1)
                        act.wait_ge(*x_done.at(l, 2))
                        mean_square(5, xres[:, 1, :])
                    if name == "ffn_gate":
                        if j >= 2:
                            act.wait_ge(*f_gate.at(l, j - 1))
                        done(activate(f_th_t[:, j % 2, :], used(name, j), ACT.Tanh, scale=0.5), f_th, j + 1)
                    split_hi(n + RING)
                    if name == "ffn_up":
                        act.wait_ge(*f_up.at(l, j + 1))
                        done(activate(two(z_hi, j % 4), pair(f_prod_t[:, j % 2, :]), ACT.Copy, scale=0.5),
                             f_hi_done, j + 1)
                    if name == "pb" and j < 3:
                        act.wait_ge(*m_done.at(l, j + 1))
                        done(activate(two(z_hi, j), two(IG, j), ACT.Copy, scale=0.5), m_hi_done, j + 1)
                    if (name, j) == ("wo", 3):
                        xa_hi(4, "h", 1, 0)
                        xa_hi(4, "h", 1, 1)
                    if (name, j) == ("gate_a", 1):
                        exps(0)
                    if (name, j) == ("gate_a", 3):
                        p_copy(0)
                        exps(1)
                    if (name, j) == ("gate_b", 1):
                        p_copy(1)
                        exps(2)
                    if (name, j) == ("gate_b", 3):
                        o_hi_part(0)
                        o_hi_part(1)
                        p_copy(2)
                        exps(3)
                    if (name, j) == ("pa", 1):
                        o_hi_part(2)
                        p_copy(3)
                    if (name, j) == ("pa", 2):
                        o_hi_part(3)
                act.wait_ge(*tile0.at(l, 2))
                mean_square(6, acc[:, 0:2, :].rearrange("p b f -> p (b f)"))
                act.wait_ge(*panel_used.at(l, NPAN))
                mean_square(7, acc[:, 2:4, :].rearrange("p b f -> p (b f)"))
                own(activate(junk[:, 0:1], eps_t[:, :], ACT.Copy))
                act.sem_clear(act_step)

        @block.vector
        def _(dve):
            v = nc.vector
            step = [0]

            def own(ins):
                step[0] += 1
                ins.then_inc(dve_step, 1)
                dve.wait_ge(dve_step, step[0])

            dve.wait_ge(vec_turned, 1)
            own(v.tensor_copy(vecs[:, :, 0:8, :], work[0][:, 0:P].rearrange("p (l v k) -> p l v k", l=DEPTH, v=8)))
            lam = vecs[:, :, 7, :]
            own(v.tensor_scalar(sp_p[:, :, :], lam, -1.0, None, ALU.mult))
            v.tensor_tensor(sp_s[:, :, :], lam, sp_p[:, :, :], ALU.max).then_inc(exp_ready, 1)

            dve.wait_ge(pos_loaded, 16)
            dve.wait_ge(consts_done, 1)
            own(v.tensor_copy(pos_f[:, :], pos_i[:, :]))
            for t in range(NT):
                own(v.tensor_scalar(ang[:, t, :], inv_freq[:, :], pos_f[:, t:t + 1], None, ALU.mult))
            two_pi, pieces = 2 * np.pi, []
            rest = two_pi
            for bits_after in (8, 19, 31, 42):
                piece = np.floor(rest * 2.0 ** bits_after) / 2.0 ** bits_after
                pieces.append(float(piece))
                rest -= piece
            magic = 1.5 * 2.0 ** 23

            def turns(n):
                unit = 2.0 ** (11 * (2 - n))
                own(v.tensor_scalar(digit[n][:, :, :], ang[:, :, :], 1.0 / (two_pi * unit), magic, ALU.mult, ALU.add))
                own(v.tensor_scalar(digit[n][:, :, :], digit[n][:, :, :], -magic, unit, ALU.add, ALU.mult))

            def less(n, piece):
                own(v.scalar_tensor_tensor(ang[:, :, :], digit[n][:, :, :], -pieces[piece], ang[:, :, :],
                                           ALU.mult, ALU.add))

            for n in range(3):
                turns(n)
                less(n, 0)
                for m in range(n + 1 if n < 2 else 0):
                    less(n - m, 1 + m)
            for n, piece in ((2, 1), (1, 2), (0, 3), (2, 2), (1, 3), (2, 3)):
                less(n, piece)
            own(v.tensor_scalar(ang[:, :, :], ang[:, :, :], 3.1415925, -3.1415925, ALU.min, ALU.max))
            own(v.tensor_scalar(digit[0][:, :, :], ang[:, :, :], -1.0, None, ALU.mult))
            own(v.tensor_tensor(digit[0][:, :, :], ang[:, :, :], digit[0][:, :, :], ALU.max))
            v.tensor_scalar(digit[0][:, :, :], digit[0][:, :, :], -1.0, float(np.pi / 2), ALU.mult,
                            ALU.add).then_inc(sines_ready, 1)

            dve.wait_ge(sinks_loaded, 16)
            by_head = sink_rows[:, :, :].rearrange("p l (g i r) -> p l g i r", i=2, r=2)
            for i in range(2):
                for par in range(2):
                    rows = slice(64 * i, 64 * i + 64)
                    own(v.tensor_copy(sinks[rows, :, 4 * par:4 * par + 4], by_head[rows, :, :, i, par]))

            dve.wait_ge(exp_done, 1)
            own(v.tensor_scalar(sp_s[:, :, :], sp_t[:, :, :], 2.0, None, ALU.add))
            own(v.reciprocal(sp_s[:, :, :], sp_s[:, :, :]))
            own(v.tensor_tensor(sp_s[:, :, :], sp_s[:, :, :], sp_t[:, :, :], ALU.mult))
            own(v.tensor_tensor(sp_t[:, :, :], sp_s[:, :, :], sp_s[:, :, :], ALU.mult))
            own(v.tensor_scalar(sp_p[:, :, :], sp_t[:, :, :], 1.0 / 17, None, ALU.mult))
            for odd in range(15, 1, -2):
                own(v.scalar_tensor_tensor(sp_p[:, :, :], sp_p[:, :, :], 1.0 / odd, sp_t[:, :, :], ALU.add, ALU.mult))
            own(v.scalar_tensor_tensor(sp_p[:, :, :], sp_p[:, :, :], 1.0, sp_s[:, :, :], ALU.add, ALU.mult))
            own(v.tensor_scalar(sp_t[:, :, :], lam, -1.0, 0.0, ALU.mult, ALU.max))
            own(v.scalar_tensor_tensor(sp_p[:, :, :], sp_p[:, :, :], 2.0, sp_t[:, :, :], ALU.mult, ALU.add))
            own(v.tensor_scalar(vecs[:, :, 8, :], sp_p[:, :, :], -LRU_C, None, ALU.mult))
            own(v.tensor_scalar(vecs[:, :, 9, :], sp_p[:, :, :], LRU_C, None, ALU.mult))
            dve.wait_ge(sines_done, 1)
            own(v.tensor_copy(pos_f[:, :], pos_i[:, :]))
            v.tensor_copy(vec[:, :, :], vecs[:, 0, :, :]).then_inc(setup_done, 1)
            dve.wait_ge(setup_done, 1)
            dve.wait_ge(x_loaded, 32)
            dve.sem_clear(dve_step)
            step[0] = 0

            with dve.Fori(0, DEPTH) as l:
                def done(ins, sig, n):
                    ins.then_inc(sig.sem, 1)
                    dve.wait_ge(*sig.at(l, n))

                def split_lo(n):
                    if n >= NPAN:
                        return
                    dve.wait_ge(*hi_done.at(l, n + 1))
                    v.tensor_tensor(w_lo[:, n % RING, :], raw[:, n % RAW, :], bits(w_hi[:, n % RING, :]),
                                    ALU.subtract).then_inc(split_done.sem, 1)

                def normed(n, i, t, gains):
                    dve.wait_ge(*rstd_done.at(l, n + 1))
                    dve.wait_ge(*pre_loaded.at(l, 16 * gains))
                    done(v.scalar_tensor_tensor(QTOK[:, t, :], xres[:, t, :], rstd[:, n:n + 1], g_pre[:, :],
                                                ALU.mult, ALU.mult), xs_done, i)

                def xa_lo(first, name, t, h):
                    m = first + 2 * t + h + 1
                    dve.wait_ge(*xa_hi_done.at(l, m))
                    cols = slice(P * t, P * t + P)
                    done(v.tensor_tensor(xn_lo[:, 4 * h:4 * h + 4, cols],
                                         bank(name, 2 * t + h)[:, :].rearrange("p (k s) -> p k s", k=4),
                                         bits(xn_hi[:, 4 * h:4 * h + 4, cols]), ALU.subtract), xa_done, m)

                def used(name, j):
                    dve.wait_ge(*panel_used.at(l, AT[name, j] + 1))
                    return bank(name, j)[:, :]

                def two(t, j):
                    return t[:, 2 * j:2 * j + 2, :]

                def pair(ps):
                    return ps.rearrange("p (k s) -> p k s", k=2)

                def conv(j):
                    dve.wait_ge(*u_done.at(l, j + 1))
                    for c in (2 * j, 2 * j + 1):
                        own(v.tensor_scalar(UC[:, c, :], U[:, c, 0:S], vec[:, 0, c:c + 1], vec[:, 4, c:c + 1],
                                            ALU.mult, ALU.add))
                        for k in range(1, CW):
                            ins = v.scalar_tensor_tensor(UC[:, c, :], U[:, c, k:k + S], vec[:, k, c:c + 1],
                                                         UC[:, c, :], ALU.mult, ALU.add)
                            if k < CW - 1:
                                own(ins)
                        done(ins, uc_done, c + 1)

                def rope(name, b, n):
                    for t in range(NT):
                        heads = 4 if name == "kv" else 8
                        width = heads * HEAD_DIM
                        ps = acc[:, b + t, 0:width]
                        dve.wait_ge(*panel_used.at(l, AT[name, 1] + 1))
                        halves = ps.rearrange("p (h i d) -> p h i d", i=2, d=32)
                        c2 = cos[:, t, :].unsqueeze(1).broadcast_to([P, 2 * heads, 32])
                        t1 = GT[:, 0, 0:width]
                        t2 = GT[:, 1, 0:width].rearrange("p (h i d) -> p h i d", i=2, d=32)
                        own(v.tensor_tensor(t1.rearrange("p (h d) -> p h d", d=32),
                                            ps.rearrange("p (h d) -> p h d", d=32), c2, ALU.mult))
                        for i in range(2):
                            s2 = sin[:, t, i, :].unsqueeze(1).broadcast_to([P, heads, 32])
                            ins = v.tensor_tensor(t2[:, :, i, :], halves[:, :, 1 - i, :], s2, ALU.mult)
                            if i == 0 or name == "kv":
                                own(ins)
                        if name == "kv":
                            vsrc = acc[:, b + t, 256:512]
                            own(v.tensor_copy(VT[:, t, :], vsrc))
                            if t == 0:
                                ins = v.tensor_copy(VS[0:64, :], acc[64:128, b, 256:512])
                            else:
                                ins = v.tensor_copy(VS[64:128, :], acc[0:64, b + 1, 256:512])
                        done(ins, rope_read, n + t + 1)
                        if name == "kv":
                            for copy in range(2):
                                ins = v.tensor_tensor(
                                    KTOK[:, t, :, 64 * copy:64 * copy + 64],
                                    t1.rearrange("p (h d) -> p h d", d=64),
                                    GT[:, 1, 0:width].rearrange("p (h d) -> p h d", d=64), ALU.add)
                                if copy == 0:
                                    own(ins)
                        else:
                            q = 512 * (name == "q1")
                            ins = v.tensor_tensor(QTOK[:, t, q:q + 512], t1, GT[:, 1, :], ALU.add)
                        done(ins, roped, n + t + 1)

                def lru_v(half):
                    cs = slice(4 * half, 4 * half + 4)
                    dve.wait_ge(*a_done.at(l, half + 1))
                    own(v.tensor_tensor(IG[:, cs, :], IG[:, cs, :], UC[:, cs, :], ALU.mult))
                    own(v.tensor_tensor(UC[:, cs, :], AG[:, cs, :], AG[:, cs, :], ALU.mult))
                    done(v.scalar_tensor_tensor(UC[:, cs, :], UC[:, cs, :], 1.0, h_lru[:, cs, :],
                                                ALU.add, ALU.mult), v_done, half + 1)

                def lru_scan(half):
                    cs = slice(4 * half, 4 * half + 4)
                    dve.wait_ge(*mult_done.at(l, half + 1))
                    own(v.tensor_tensor(IG[:, cs, :], IG[:, cs, :], UC[:, cs, :], ALU.mult))
                    for c in range(4 * half, 4 * half + 4):
                        ins = v.tensor_tensor_scan(h_lru[:, c, :], AG[:, c, :], IG[:, c, :], 0.0, ALU.mult, ALU.add)
                        if c % 4 < 3:
                            own(ins)
                    done(ins, h_done, half + 1)

                def gelu_inner(j):
                    dve.wait_ge(*g_sq.at(l, j + 1))
                    g = GT[:, j % 2, :]
                    own(v.tensor_scalar(g, g, GELU_CUBE, 1.0, ALU.mult, ALU.add))
                    done(v.tensor_tensor(g, g, bank("gelu", j)[:, :], ALU.mult), g_in, j + 1)

                def gelu_outer(j):
                    dve.wait_ge(*g_th.at(l, j + 1))
                    g = GT[:, j % 2, :]
                    done(v.scalar_tensor_tensor(g, g, 1.0, bank("gelu", j)[:, :], ALU.add, ALU.mult), g_read, j + 1)

                def z_part(j):
                    g = pair(GT[:, j % 2, :])
                    done(v.scalar_tensor_tensor(g, g, 0.5, two(h_lru, j), ALU.mult, ALU.mult), z_done, j + 1)
                    dve.wait_ge(*z_hi_done.at(l, j + 1))
                    done(v.tensor_tensor(two(z_lo, j), g, bits(two(z_hi, j)), ALU.subtract), z_lo_done, j + 1)

                def softmax(c):
                    _, nk = key_span(c)
                    for par in range(2 if c == 0 else 0):
                        own(v.memset(prob(c, par)[:, :, :, nk:], 0.0))
                    for par in range(2):
                        u = 2 * c + par
                        dve.wait_ge(*scored.at(l, u + 1))
                        own(v.tensor_reduce(sm[:, u, 0, :], acc[:, par, :].rearrange("p (g k) -> p g k", g=4)[:, :, 0:nk],
                                            AX.X, ALU.max))
                        own(v.scalar_tensor_tensor(sm[:, u, 1, :], sm[:, u, 0, :], HEAD_DIM ** -0.5,
                                                   sink[:, 4 * par:4 * par + 4], ALU.mult, ALU.max))
                        own(v.tensor_scalar(sm[:, u, 2, :], sm[:, u, 1, :], -1.0, None, ALU.mult))
                        done(v.tensor_tensor(sm[:, u, 4, :], sink[:, 4 * par:4 * par + 4], sm[:, u, 2, :], ALU.add),
                             bias_done, u + 1)
                    for par in range(2):
                        u = 2 * c + par
                        dve.wait_ge(*sink_exp.at(l, u + 1))
                        own(v.tensor_tensor(sm[:, u, 6, :], sm[:, u, 3, :], sm[:, u, 5, :], ALU.add))
                        own(v.reciprocal(sm[:, u, 7, :], sm[:, u, 6, :]))
                        inv = sm[:, u, 7, :].rearrange("p (r h) -> p r h", h=2).unsqueeze(3)
                        p = prob(c, par)[:, :, :, 0:nk]
                        done(v.tensor_tensor(p, p, inv.broadcast_to([P, 2, 2, nk]), ALU.mult), p_done, u + 1)

                def o_lo_part(c):
                    dve.wait_ge(*o_hi_done.at(l, c + 1))
                    cols = slice(CHUNK * c, CHUNK * c + CHUNK)
                    done(v.tensor_tensor(xn_lo[:, :, cols], bank("pv", c)[:, :].rearrange("p (k s) -> p k s", k=KD),
                                         bits(xn_hi[:, :, cols]), ALU.subtract), o_done, c + 1)

                def add_branch(n, i, t, gains):
                    dve.wait_ge(*rstd_done.at(l, n + 1))
                    dve.wait_ge(*post_loaded.at(l, 16 * gains))
                    tmp = QT[:, 4 * t:4 * t + 4, :].rearrange("p k s -> p (k s)")
                    done(v.scalar_tensor_tensor(tmp, acc[:, 2 * t:2 * t + 2, :].rearrange("p b f -> p (b f)"),
                                                rstd[:, n:n + 1], g_post[:, :], ALU.mult, ALU.mult), branch_read, i)
                    done(v.tensor_tensor(xres[:, t, :], xres[:, t, :], tmp, ALU.add), x_done, i)

                own(v.tensor_copy(vec[:, :, :], vecs[:, bass.ds(l, 1), :, :].rearrange("p o v k -> p (o v) k")))
                own(v.tensor_copy(sink[:, :], sinks[:, bass.ds(l, 1), :].rearrange("p o h -> p (o h)")))
                normed(0, 1, 0, 1)
                normed(1, 2, 1, 1)
                split_lo(0)
                for t in range(NT):
                    for h in range(2):
                        xa_lo(0, "xn", t, h)
                for n in range(1, RING):
                    split_lo(n)

                for n, (name, j) in enumerate(PLAN):
                    if name == "u":
                        conv(j)
                    if (name, j) == ("kv", 1):
                        rope("kv", 0, 0)
                    if (name, j) == ("q0", 1):
                        rope("q0", 2, 2)
                    if (name, j) == ("q1", 1):
                        rope("q1", 0, 4)
                    if name == "gelu":
                        if j >= 2:
                            z_part(j - 2)
                        gelu_inner(j)
                        if j < 2:
                            lru_v(j)
                        gelu_outer(j)
                        if j == 1:
                            lru_scan(0)
                            lru_scan(1)
                    if (name, j) == ("gate_a", 0):
                        z_part(2)
                        z_part(3)
                    if name == "pa":
                        dve.wait_ge(*gate_th.at(l, j + 1))
                        ps = used("pa", j)
                        done(v.scalar_tensor_tensor(two(IG, j), two(thA, j), 1.0, pair(ps), ALU.add, ALU.mult),
                             ya_read, j + 1)
                    if name == "pb":
                        dve.wait_ge(*gate_th.at(l, j + 5))
                        ps = used("pb", j)
                        g = pair(GT[:, j % 2, :])
                        done(v.scalar_tensor_tensor(g, two(thB, j), 1.0, pair(ps), ALU.add, ALU.mult),
                             yb_read, j + 1)
                        done(v.tensor_tensor(two(IG, j), two(IG, j), g, ALU.add), m_done, j + 1)
                    if (name, j) == ("wo", 0):
                        add_branch(2, 1, 0, 1)
                        normed(3, 3, 0, 2)
                    if (name, j) == ("wo", 3):
                        add_branch(4, 2, 1, 1)
                        xa_lo(4, "h", 0, 0)
                        xa_lo(4, "h", 0, 1)
                        normed(5, 4, 1, 2)
                    if name == "ffn_gate":
                        dve.wait_ge(*f_th.at(l, j + 1))
                        done(v.scalar_tensor_tensor(f_silu_t[:, j % 2, :], f_th_t[:, j % 2, :], 1.0,
                                                    bank(name, j)[:, :], ALU.add, ALU.mult), f_gate, j + 1)
                    if name == "ffn_up":
                        done(v.tensor_tensor(f_prod_t[:, j % 2, :], f_silu_t[:, j % 2, :], used(name, j), ALU.mult),
                             f_up, j + 1)
                    if (name, j) != ("pb", 3):
                        split_lo(n + RING)
                    if name == "pb":
                        dve.wait_ge(*m_hi_done.at(l, j + 1))
                        done(v.scalar_tensor_tensor(two(z_lo, j), two(IG, j), 0.5, bits(two(z_hi, j)), ALU.mult,
                                                    ALU.subtract), m_lo_done, j + 1)
                        if j == 3:
                            split_lo(n + RING)
                    if name == "ffn_up":
                        dve.wait_ge(*f_hi_done.at(l, j + 1))
                        done(v.scalar_tensor_tensor(two(z_lo, j % 4), pair(f_prod_t[:, j % 2, :]), 0.5,
                                                    bits(two(z_hi, j % 4)), ALU.mult, ALU.subtract), f_done, j + 1)
                    if (name, j) == ("wo", 3):
                        xa_lo(4, "h", 1, 0)
                        xa_lo(4, "h", 1, 1)
                    if (name, j) == ("gate_a", 1):
                        softmax(0)
                    if (name, j) == ("gate_a", 3):
                        softmax(1)
                    if (name, j) == ("gate_b", 1):
                        softmax(2)
                    if (name, j) == ("gate_b", 3):
                        o_lo_part(0)
                        o_lo_part(1)
                        softmax(3)
                    if (name, j) == ("pa", 1):
                        o_lo_part(2)
                    if (name, j) == ("pa", 2):
                        o_lo_part(3)
                add_branch(6, 3, 0, 2)
                add_branch(7, 4, 1, 2)
                own(v.tensor_copy(sm[:, 0, 0, 0:1], eps_t[:, :]))
                dve.sem_clear(dve_step)


INS = ["x", "positions", "pre_mix_g", "w_in", "conv_w", "conv_b", "lru_wa", "lru_ba", "lru_wx", "lru_bx",
       "lru_lambda", "attn_sinks", "w_pa", "w_pb", "w_o", "post_mix_g", "pre_ffn_g", "w_ffn_gate",
       "w_ffn_up", "w_ffn_down", "post_ffn_g"]


def kernel(**inputs):
    import concourse.bacc as bacc
    from concourse.bass_utils import run_bass_kernel_spmd

    nc = bacc.Bacc("TRN2", target_bir_lowering=False, num_devices=1)
    arrays, args = {}, []
    for name in INS:
        a = np.ascontiguousarray(inputs[name])
        arrays[f"in_{name}"] = a
        args.append(nc.dram_tensor(f"in_{name}", a.shape, mybir.dt.from_np(a.dtype), kind="ExternalInput").ap())
    shape = inputs["x"].shape
    args.append(nc.dram_tensor("out_0", shape, F32, kind="ExternalOutput").ap())
    trunk(nc, *args)
    result = run_bass_kernel_spmd(nc, [arrays], core_ids=[0])
    return result.results[0]["out_0"]
```

```python
from contextlib import ExitStack

import numpy as np

import concourse.bass as bass
from concourse import mybir

P = 128
F32 = mybir.dt.float32
F32R = mybir.dt.float32r
I32 = mybir.dt.int32
ALU = mybir.AluOpType
ACT = mybir.ActivationFunctionType
AX = mybir.AxisListType

HEAD_DIM = 64
CHUNK = 64
ROPE_THETA = 10000.0
LRU_C = 8.0
EPS = 1e-6
GELU_CUBE = 0.044715
GELU_SCALE = 0.7978845608028654

RAW = 3
RING = 4
PANEL = 2048


class Signal:

    def __init__(self, sem, per_layer, start=0):
        self.sem, self.per_layer, self.start = sem, per_layer, start

    def at(self, layer, n):
        assert 1 <= n <= self.per_layer
        return self.sem, layer * self.per_layer + (self.start + n)


def panel_plan(groups):
    plan = [("kv", 0), ("kv", 1), ("q0", 0), ("q0", 1)]
    plan += [("u", j) for j in range(4)] + [("q1", 0), ("q1", 1)]
    for name in ("gate_a", "gelu", "gate_b", "pa", "pb", "wo"):
        plan += [(name, j) for j in range(4)]
    for c in range(groups):
        plan += [("fg", 2 * c), ("fg", 2 * c + 1), ("fu", 2 * c), ("fu", 2 * c + 1)]
        if c:
            plan += [("down", 2 * c - 2), ("down", 2 * c - 1)]
    plan.remove(("down", 2 * groups - 3))
    plan += [("fgu", 0), ("fgu", 1)]
    plan += [("down", j) for j in range(2 * groups - 3, 2 * groups + 1)]
    return plan


def work_bank_uses(groups):
    def four(name):
        return [(name, n) for n in range(4)]

    uses = four("xn") + [("u", 0), ("u", 1), ("u", 2), ("gates", 0), ("gates", 1), ("u", 3)]
    uses += [("gates", 2), ("gates", 3)] + [("gates", c) for c in range(4, 8)] + four("gate_a")
    uses += four("gelu") + four("gate_b")
    uses += [("pv", 0), ("pv", 1), ("pa", 0), ("pa", 1), ("pv", 2), ("pv", 3)]
    uses += [("pa", 2), ("pa", 3), ("pb", 0), ("pb", 1), ("pb", 2), ("turn_m", 0)]
    uses += [("turn_m", 1), ("pb", 3), ("turn_m", 2), ("turn_m", 3)]
    uses += [("h", 0), ("h", 1), ("fg", 0), ("fu", 0), ("h", 2), ("h", 3), ("fg", 1), ("fu", 1)]
    for c in range(1, groups):
        uses += [(name, 2 * d + t) for name, d in (("fg", c), ("fu", c), ("turn_f", c - 1)) for t in range(2)]
    n = 2 * groups
    return uses + [("fgu", 0), ("fgu", 1), ("turn_f", n - 2), ("turn_f", n - 1), ("turn_f", n)]


def trunk(nc, x, positions, pre_mix_g, w_in, conv_w, conv_b, lru_wa, lru_ba, lru_wx, lru_bx,
          lru_lambda, attn_sinks, w_pa, w_pb, w_o, post_mix_g, pre_ffn_g, w_ffn_gate, w_ffn_up,
          w_ffn_down, post_ffn_g, out):
    _, S, D = x.shape
    DEPTH = w_in.shape[0]
    NT = S // P
    KD = D // P
    GROUPS = w_ffn_gate.shape[2] // 512
    TAIL_COL = 512 * GROUPS
    NH = attn_sinks.shape[1]
    NC = S // CHUNK
    CW = conv_w.shape[1]
    assert (S, D, NT, KD, NH, NC, CW) == (256, 1024, 2, 8, 16, 4, 4)
    assert w_ffn_gate.shape[2] == TAIL_COL + 256
    PLAN = panel_plan(GROUPS)
    NPAN = len(PLAN)
    AT = {name: n for n, name in enumerate(PLAN)}
    COL_U, COL_G, COL_Q, COL_KV, COL_GA, COL_GB = 0, 1024, 2048, 3072, 3584, 4608

    with ExitStack() as ctx:
        def sb(name, shape, dt=F32):
            return ctx.enter_context(nc.sbuf_tensor(name, shape, dt))

        def sem(name):
            return ctx.enter_context(nc.semaphore(name))

        def signal(name, per_layer, start=0):
            return Signal(sem(name), per_layer, start)

        raw = sb("weights_raw", [P, RAW, PANEL])
        w_hi = sb("weights_hi", [P, RING, PANEL], F32R)
        w_lo = sb("weights_lo", [P, RING, PANEL], F32R)
        XA = [sb(f"act_a_{s}", [P, KD, S], F32R) for s in ("hi", "lo")]
        XB = [sb(f"act_b_{s}", [P, KD, S], F32R) for s in ("hi", "lo")]
        xres = sb("x_residual", [P, NT, D])
        g_pre = sb("gain_pre", [P, D])
        g_post = sb("gain_post", [P, D])
        U = sb("lru_u", [P, KD, S + CW - 1])
        UC = sb("lru_uc", [P, KD, S])
        IG = sb("lru_i", [P, KD, S])
        AG = sb("lru_a", [P, KD, S])
        QTOK = sb("q_tok", [P, NT, D])
        KTOK = sb("k_tok", [P, NT, 4, P])
        VT = sb("v_tok", [P, NT, 256])
        VS = sb("v_shifted", [P, 256])
        QT = sb("q_feat", [P, KD, S])
        KT = sb("k_feat", [P, 4, S])
        GT = sb("temps", [P, 2, 512])
        ident = sb("identity", [P, P])
        vec_rows = sb("vector_rows", [DEPTH * 8 * KD, P])
        vecs = sb("vectors", [P, DEPTH, 10, KD])
        vec = sb("vectors_of_layer", [P, 10, KD])
        sink_rows = sb("sink_rows", [P, DEPTH, NH])
        sinks = sb("sinks", [P, DEPTH, 2, 8])
        sink = sb("sinks_of_layer", [P, 2, 8])
        pos_i = sb("pos_int", [P, NT], I32)
        pos_f = sb("pos_float", [P, NT])
        inv_freq = sb("inv_freq", [P, 32])
        ang = sb("angle", [P, NT, 32])
        digit = [sb(f"turns_{n}", [P, NT, 32]) for n in range(3)]
        turned_by = sb("turned_by", [P, NT, 32])
        cos = sb("cos", [P, NT, 32])
        sin = sb("sin_signed", [P, NT, 2, 32])
        sp_t = sb("softplus_t", [P, DEPTH, KD])
        sp_s = sb("softplus_s", [P, DEPTH, KD])
        sp_p = sb("softplus_p", [P, DEPTH, KD])
        mean_sq = sb("mean_square", [P, 8])
        ms_eps = sb("mean_square_eps", [P, 8])
        rstd = sb("rstd", [P, 8])
        eps_t = sb("eps", [P, 1])
        idle = sb("unread", [P, 1])
        mhalf = sb("minus_half", [P, 1])
        sm = sb("softmax_small", [P, 4, 6, 8])

        def bits(ap):
            return ap.bitcast(F32)

        def t_panel(ring, slot, kc):
            return ring[:, slot, :].rearrange("p (k f) -> p k f", k=kc)

        xn_hi, xn_lo = XA
        z_hi, z_lo = XB
        thA = QTOK
        bd_a, bd_x = (QT[:, k:k + 4, :].rearrange("p a (b d) -> p (a b) d", b=2) for k in (0, 4))
        junk = KTOK[:, :, :, :].rearrange("p t g d -> p (t g d)")
        h_lru = U[:, :, CW - 1:]
        merged = IG[:, :, :].rearrange("p (t k) s -> p t (k s)", t=NT)
        f_th_t = IG[:, 0:4, :].rearrange("p (t k) s -> p t (k s)", t=NT)
        f_silu_t = IG[:, 4:8, :].rearrange("p (t k) s -> p t (k s)", t=NT)
        f_prod_t = UC[:, :, :].rearrange("p (b k) s -> p b (k s)", b=4)

        def thB(c, t):
            k = 4 * t + 2 * c
            return U[:, k:k + 2, CW - 1:]

        q_rows = QT[:, :, :].rearrange("p (c a) s -> p c (a s)", c=NC)

        def prob(c):
            if c % 2 == 0:
                return KTOK[:, :, :, :]
            return AG[:, 0:4, :].rearrange("p a s -> p (a s)").rearrange("p (r g k) -> p r g k", r=2, g=4)

        def prob_t(c):
            return UC[:, 4 * (c % 2):4 * (c % 2) + 4, :].rearrange("p a (h k) -> p (a h) k", h=2)

        def key_span(c):
            return (0, CHUNK) if c == 0 else (CHUNK * (c - 1), 2 * CHUNK)

        work = [ctx.enter_context(nc.psum_tensor(f"work_{b}", [P, 512], F32)) for b in range(4)]
        acc = ctx.enter_context(nc.psum_tensor("acc", [P, 4, 512], F32))

        SLOT, BEFORE, LAST_OF, slot = [], [], {}, 0
        skips = [AT["fg", 2 * c] for c in range(2, 2 + -NPAN % RING)]
        for n in range(NPAN):
            slot += n in skips
            SLOT.append(slot % RING)
            BEFORE.append(LAST_OF.get(slot % RING))
            LAST_OF[slot % RING] = n
            slot += 1
        assert slot % RING == 0
        SPLIT_AT = {n: [m for m in range(RING, NPAN) if max(m - RING, BEFORE[m]) == n] for n in range(NPAN)}
        LOADED, total = [], [0] * RAW
        for n, (name, _) in enumerate(PLAN):
            total[n % RAW] += 32 if name == "fgu" else 16
            LOADED.append(total[n % RAW])

        raw_loaded = [signal(f"raw_loaded_{s}", total[s]) for s in range(RAW)]
        hi_done = signal("panel_hi_done", NPAN)
        split_done = signal("panel_split_done", NPAN)
        panel_used = signal("panel_used", NPAN)
        bd_loaded = signal("blockdiag_loaded", 64)
        pre_loaded = signal("gain_pre_loaded", 32)
        post_loaded = signal("gain_post_loaded", 32)
        ms_done = signal("mean_square_done", 8, 2)
        rstd_done = signal("rstd_done", 8, 2)
        xs_done = signal("normed_tile_done", 4)
        turned = signal("x_turned", 8)
        xa_hi_done = signal("xa_hi_done", 8)
        xa_done = signal("xa_done", 8)
        u_done = signal("u_copied", 4)
        tap_done = signal("first_tap_done", 8)
        uc_done = signal("conv_done", 8)
        gates_mm = signal("gates_multiplied", 8)
        gates_done = signal("gate_sigmoids_done", 8)
        a_done = signal("decay_done", 2)
        v_done = signal("mult_square_done", 2)
        mult_done = signal("mult_done", 2)
        h_done = signal("scan_done", 2)
        roped = signal("rope_done", 6)
        rope_read = signal("rope_psum_read", 6)
        qk_turned = signal("qk_turned", 6)
        qk_done = signal("qk_feat_done", 6)
        g_sq = signal("gelu_square", 4)
        g_in = signal("gelu_inner", 4)
        g_th = signal("gelu_tanh", 4)
        g_read = signal("gelu_psum_read", 4)
        z_done = signal("z_done", 4)
        z_hi_done = signal("z_hi_done", 4)
        z_lo_done = signal("z_lo_done", 4)
        gate_th = signal("merge_gate_tanh", 8)
        scored = signal("scores_multiplied", 8)
        bias_done = signal("softmax_bias_done", 4)
        score_read = signal("scores_read", 8)
        sink_exp = signal("sink_exp_done", 4)
        p_done = signal("p_done", 4)
        p_turned = signal("p_turned", 8)
        pt_done = signal("p_feat_done", 8)
        pv = signal("pv_multiplied", 4)
        o_hi_done = signal("o_hi_done", 4)
        o_done = signal("o_done", 4)
        ya_read = signal("ya_read", 4)
        yb_read = signal("yb_read", 4)
        m_done = signal("mixed_done", 4)
        m_turned = signal("mixed_turned", 4)
        m_hi_done = signal("mixed_hi_done", 4)
        m_lo_done = signal("mixed_lo_done", 4)
        tile0 = signal("first_tile_multiplied", 7)
        branch_read = signal("branch_psum_read", 4)
        x_done = signal("x_updated", 4)
        f_th = signal("silu_tanh", 2 * GROUPS + 2)
        f_gate = signal("silu_done", 2 * GROUPS + 2)
        f_up = signal("ffn_product_done", 2 * GROUPS + 2)
        f_turned = signal("ffn_turned", 2 * GROUPS + 1)
        f_hi_done = signal("ffn_hi_done", 2 * GROUPS + 1)
        f_done = signal("ffn_done", 2 * GROUPS + 1)
        x_loaded = [sem(f"x_loaded_{t}") for t in range(NT)]
        rows_loaded, pos_loaded, sinks_loaded, history_done = (
            sem(n) for n in ("rows_loaded", "pos_loaded", "sinks_loaded", "history_done"))
        cleared = signal("blockdiag_cleared", 2)
        ident_done, pos_done = (sem(n) for n in ("ident_done", "pos_done"))
        angle_done = sem("angle_done")
        vec_turned, vec_copied, sines_ready, sines_done, exp_ready, exp_done = (
            sem(n) for n in ("vec_turned", "vec_copied", "sines_ready", "sines_done", "exp_ready", "exp_done"))
        dve_step, act_step, pool_step, stored = (
            sem(n) for n in ("dve_step", "act_step", "pool_step", "stored"))

        USES = work_bank_uses(GROUPS)
        USE = {name: n for n, name in enumerate(USES)}
        FREED_BY = {"xn": (xa_done, 0), "u": (u_done, 0), "gates": (gates_done, 0),
                    "gelu": (g_read, 0), "gate_a": (gate_th, 0), "gate_b": (gate_th, 4),
                    "pv": (o_done, 0), "pa": (ya_read, 0), "pb": (yb_read, 0), "turn_m": (m_lo_done, 0),
                    "h": (xa_done, 4), "fg": (f_gate, 0), "fu": (f_up, 0), "fgu": (f_up, 2 * GROUPS),
                    "turn_f": (f_done, 0)}

        def bank(name, n):
            if name == "turn":
                return acc[:, 2 + n % 2, :]
            return work[USE[name, n] % 4]

        def multiplied(name, c, t):
            first = {("kv", 0): 1, ("q0", 0): 2, ("pb", 1): 3, ("fg", 0): 5, ("fu", 0): 6}.get((name, c))
            if t == 0 and first:
                return tile0, first
            return panel_used, AT[name, 2 * c + 1] + 1

        SCORES_AT = [("gelu", 0), ("gelu", 2), ("gate_b", 0), ("gate_b", 2)]
        SOFTMAX_AT = [("gelu", 1), ("gelu", 3), ("gate_b", 1), ("gate_b", 3)]

        NORM_ORDER = [2, 3, 4, 5, 6, 0, 7, 1]

        def for_layers(eng, layer):
            if DEPTH > 1:
                with eng.Fori(0, DEPTH - 1) as l:
                    layer(l, False)
            layer(DEPTH - 1, True)

        block = ctx.enter_context(nc.Block())

        @block.sync
        def _(sp):
            def load(l, n):
                name, j = PLAN[n]
                sig, slot = raw_loaded[n % RAW].sem, raw[:, n % RAW, :]
                if name == "fgu":
                    dst = slot.rearrange("p (k f) -> p k f", k=4)
                    for i, w in enumerate((w_ffn_gate, w_ffn_up)):
                        src = w[l][512 * j:512 * j + 512, TAIL_COL:TAIL_COL + 256]
                        sp.dma_start(dst[:, :, 256 * i:256 * i + 256],
                                     src.rearrange("(k p) f -> p k f", p=P)).then_inc(sig, 16)
                    return
                if name in ("u", "gelu"):
                    c = {"u": COL_U, "gelu": COL_G}[name] + 256 * j
                    src = w_in[l][:, c:c + 256]
                elif name in ("wo", "down"):
                    src = (w_o if name == "wo" else w_ffn_down)[l][256 * j:256 * j + 256, :]
                else:
                    w, c = {"kv": (w_in, COL_KV), "q0": (w_in, COL_Q), "q1": (w_in, COL_Q + 512),
                            "gate_a": (w_in, COL_GA), "gate_b": (w_in, COL_GB), "pa": (w_pa, 0),
                            "pb": (w_pb, 0), "fg": (w_ffn_gate, 0), "fu": (w_ffn_up, 0)}[name]
                    c += 512 * (j // 2)
                    src = w[l][512 * (j % 2):512 * (j % 2) + 512, c:c + 512]
                sp.dma_start(slot.rearrange("p (k f) -> p k f", k=src.shape[0] // P),
                             src.rearrange("(k p) f -> p k f", p=P)).then_inc(sig, 16)

            sp.dma_start(xres[:, 0, :], x[0, 0:P, :]).then_inc(x_loaded[0], 16)
            sp.dma_start(g_pre[:, :], pre_mix_g[0].partition_broadcast(P)).then_inc(pre_loaded.sem, 16)
            load(0, 0)
            sp.dma_start(xres[:, 1, :], x[0, P:S, :]).then_inc(x_loaded[1], 16)
            for i, part in enumerate((conv_w.rearrange("l c (k p) -> (l c k) p", p=P),
                                      conv_b.rearrange("l (k p) -> (l k) p", p=P),
                                      lru_ba.rearrange("l (k b) e -> (l k) (b e)", b=2),
                                      lru_bx.rearrange("l (k b) e -> (l k) (b e)", b=2),
                                      lru_lambda.rearrange("l (k p) -> (l k) p", p=P))):
                row = (0 if i == 0 else CW + i - 1) * DEPTH * KD
                sp.dma_start(vec_rows[row:row + part.shape[0], :], part).then_inc(rows_loaded, 16)
            for n in range(1, RAW):
                load(0, n)

            def layer(l, last):
                for n in range(RAW, NPAN):
                    sp.wait_ge(*split_done.at(l, n - RAW + 1))
                    load(l, n)
                    if n == RAW:
                        sp.wait_ge(*cleared.at(l, 2))
                        for b in range(2):
                            for dst, src in ((bd_a, lru_wa), (bd_x, lru_wx)):
                                sp.dma_start(dst[64 * b:64 * b + 64, :, 64 * b:64 * b + 64],
                                             src[l].rearrange("(k b) d e -> b d k e", b=2)[b]
                                             ).then_inc(bd_loaded.sem, 16)
                    if n == 4 + RING + RAW:
                        sp.dma_start(g_pre[:, :], pre_ffn_g[l].partition_broadcast(P)).then_inc(pre_loaded.sem, 16)
                        sp.dma_start(g_post[:, :], post_mix_g[l].partition_broadcast(P)).then_inc(post_loaded.sem, 16)
                    if n == AT["fg", 2] + RING + RAW:
                        sp.dma_start(g_post[:, :], post_ffn_g[l].partition_broadcast(P)).then_inc(post_loaded.sem, 16)
                        if not last:
                            sp.dma_start(g_pre[:, :], pre_mix_g[l + 1].partition_broadcast(P)
                                         ).then_inc(pre_loaded.sem, 16)
                if not last:
                    for n in range(RAW):
                        sp.wait_ge(*split_done.at(l, 1 + max(m for m in range(NPAN) if m % RAW == n)))
                        load(l + 1, n)

            for_layers(sp, layer)
            for t in range(NT):
                sp.wait_ge(*x_done.at(DEPTH - 1, 3 + t))
                sp.dma_start(out[0, P * t:P * t + P, :], xres[:, t, :]).then_inc(stored, 16)
            sp.wait_ge(stored, 32)

        @block.gpsimd
        def _(pool):
            nc.gpsimd.memset(ident[:, :], 0.0).then_inc(pool_step, 1)
            nc.gpsimd.memset(eps_t[:, :], EPS).then_inc(pool_step, 1)
            nc.gpsimd.memset(mhalf[:, :], -0.5).then_inc(pool_step, 1)
            pool.wait_ge(pool_step, 1)
            nc.gpsimd.affine_select(out=ident[:, :], in_=ident[:, :], compare_op=ALU.not_equal, fill=1.0,
                                    base=0, pattern=[[-1, P]], channel_multiplier=1).then_inc(ident_done, 1)
            pool.wait_ge(pool_step, 3)
            steps = [3]

            def own(ins):
                steps[0] += 1
                ins.then_inc(pool_step, 1)
                pool.wait_ge(pool_step, steps[0])

            def rstd_of(n, ready, count):
                pool.wait_ge(*ready)
                nc.gpsimd.tensor_tensor(ms_eps[:, n:n + 1], mean_sq[:, n:n + 1], eps_t[:, :],
                                        ALU.add).then_inc(pool_step, 1)
                pool.wait_ge(pool_step, count)
                nc.gpsimd.tensor_tensor(rstd[:, n:n + 1], ms_eps[:, n:n + 1], mhalf[:, :],
                                        ALU.pow).then_inc(rstd_done.sem, 1)

            for i, v in enumerate(ROPE_THETA ** (-np.arange(0, HEAD_DIM, 2) / HEAD_DIM)):
                ins = nc.gpsimd.memset(inv_freq[:, i:i + 1], float(v))
            own(ins)
            nc.gpsimd.memset(bd_a, 0.0).then_inc(cleared.sem, 1)
            nc.gpsimd.memset(bd_x, 0.0).then_inc(cleared.sem, 1)
            steps[0] += 1
            rstd_of(0, (ms_done.sem, 1), steps[0])

            g = nc.gpsimd
            pool.wait_ge(pos_done, 1)
            for t in range(NT):
                own(g.tensor_scalar(ang[:, t, :], inv_freq[:, :], pos_f[:, t:t + 1], None, ALU.mult))
            two_pi, pieces = 2 * np.pi, []
            rest = two_pi
            for bits_after in (8, 19, 31, 42):
                piece = np.floor(rest * 2.0 ** bits_after) / 2.0 ** bits_after
                pieces.append(float(piece))
                rest -= piece
            magic = 1.5 * 2.0 ** 23

            def turns(n):
                unit = 2.0 ** (11 * (2 - n))
                own(g.tensor_scalar(digit[n][:, :, :], ang[:, :, :], 1.0 / (two_pi * unit), magic, ALU.mult, ALU.add))
                own(g.tensor_scalar(digit[n][:, :, :], digit[n][:, :, :], -magic, unit, ALU.add, ALU.mult))

            def less(n, piece):
                own(g.tensor_scalar(turned_by[:, :, :], digit[n][:, :, :], pieces[piece], None, ALU.mult))
                ins = g.tensor_tensor(ang[:, :, :], ang[:, :, :], turned_by[:, :, :], ALU.subtract)
                if (n, piece) == (2, 3):
                    ins.then_inc(angle_done, 1)
                else:
                    own(ins)

            for n in range(3):
                turns(n)
                less(n, 0)
                for m in range(n + 1 if n < 2 else 0):
                    less(n - m, 1 + m)
                if n == 0:
                    steps[0] += 1
                    rstd_of(1, (ms_done.sem, 2), steps[0])
            for n, piece in ((2, 1), (1, 2), (0, 3), (2, 2), (1, 3), (2, 3)):
                less(n, piece)
            base = steps[0]
            nc.gpsimd.memset(U[:, :, 0:CW - 1], 0.0).then_inc(history_done, 1)
            pool.wait_ge(history_done, 1)

            def layer(l, last):
                for c in range(KD):
                    if c % 2 == 0:
                        pool.wait_ge(*u_done.at(l, c // 2 + 1))
                    nc.gpsimd.tensor_scalar(UC[:, c, :], U[:, c, 0:S], vec[:, 0, c:c + 1], vec[:, 4, c:c + 1],
                                            ALU.mult, ALU.add).then_inc(tap_done.sem, 1)
                for m, n in enumerate(NORM_ORDER[:4] + [6, 7] if last else NORM_ORDER):
                    rstd_of(n, ms_done.at(l, m + 1), l * 8 + (base + 1 + m))
                if not last:
                    pool.wait_ge(*x_done.at(l, 4))
                    nc.gpsimd.memset(bd_a, 0.0).then_inc(cleared.sem, 1)
                    nc.gpsimd.memset(bd_x, 0.0).then_inc(cleared.sem, 1)

            for_layers(pool, layer)

        @block.tensor
        def _(pe):
            mm = nc.tensor.matmul

            def turn_x(l, first, name, t):
                for h in range(2):
                    dst = claim(l, name, 2 * t + h)
                    if h == 0:
                        pe.wait_ge(*xs_done.at(l, first // 2 + t + 1))
                    for k in range(4):
                        f = (4 * h + k) * P
                        last = nc.tensor.transpose(dst[:, k * P:k * P + P], QTOK[:, t, f:f + P], ident[:, :])
                    last.then_inc(turned.sem, 1)

            def claim(l, name, n):
                k = USE[name, n]
                if k >= 4:
                    before, m = USES[k - 4]
                    freed, first = FREED_BY[before]
                    pe.wait_ge(*freed.at(l, first + m + 1))
                return work[k % 4]

            pe.wait_ge(ident_done, 1)
            turn_x(0, 0, "xn", 0)
            pe.wait_ge(rows_loaded, 16 * 5)
            nc.tensor.transpose(acc[:, 3, 0:P], vec_rows[:, :], ident[:, :]).then_inc(vec_turned, 1)

            def layer(l, last_layer):
                def split_ready(n):
                    pe.wait_ge(*split_done.at(l, n + 1))

                def f_product(name, j, hi, lo):
                    n = AT[name, j]
                    dst = claim(l, name, j)
                    split_ready(n)
                    wh, wl = t_panel(w_hi, SLOT[n], KD), t_panel(w_lo, SLOT[n], KD)
                    for c in range(2):
                        o = dst[:, c * S:c * S + S]
                        for k in range(KD):
                            h, w = wh[:, k, c * P:c * P + P], wl[:, k, c * P:c * P + P]
                            mm(o, h, hi[:, k, :], start=k == 0, stop=False)
                            mm(o, h, lo[:, k, :], start=False, stop=False)
                            last = mm(o, w, hi[:, k, :], start=False, stop=k == KD - 1)
                    last.then_inc(panel_used.sem, 1)

                def t_products(dst, hi, lo, k, t, wh, wl, first, final):
                    xh, xl = hi[:, k, t * P:t * P + P], lo[:, k, t * P:t * P + P]
                    mm(dst, xh, wh, start=first, stop=False)
                    mm(dst, xh, wl, start=False, stop=False)
                    return mm(dst, xl, wh, start=False, stop=final)

                def t_panel_product(name, j, dst, hi, lo, t):
                    n = AT[name, j]
                    wh, wl = t_panel(w_hi, SLOT[n], 4), t_panel(w_lo, SLOT[n], 4)
                    for k in range(4):
                        last = t_products(dst, hi, lo, 4 * (j % 2) + k, t, wh[:, k, :], wl[:, k, :],
                                          j % 2 == 0 and k == 0, j % 2 == 1 and k == 3)
                    return last

                def t_product(name, j, dsts, hi, lo):
                    split_ready(AT[name, j])
                    for t in range(NT):
                        last = t_panel_product(name, j, dsts[t], hi, lo, t)
                    last.then_inc(panel_used.sem, 1)

                def t_pair(name, c, hi, lo, between=None):
                    dsts = [claim(l, name, 2 * c + t)[:, :] for t in range(NT)]
                    t_product(name, 2 * c, dsts, hi, lo)
                    if between:
                        between()
                    t_product(name, 2 * c + 1, dsts, hi, lo)

                def tile_pass(t, parts, hi, lo, before_last=None):
                    for i, (name, j0, dst) in enumerate(parts):
                        for j in (j0, j0 + 1):
                            if before_last and i == len(parts) - 1 and j == j0 + 1:
                                before_last()
                            if t == 0:
                                split_ready(AT[name, j])
                            last = t_panel_product(name, j, dst, hi, lo, t)
                            if t == NT - 1:
                                last.then_inc(panel_used.sem, 1)
                        if t == 0:
                            last.then_inc(tile0.sem, 1)

                def row_panel(n, k0, hi, lo, t, first, final):
                    wh, wl = t_panel(w_hi, SLOT[n], 2), t_panel(w_lo, SLOT[n], 2)
                    for kk in range(2):
                        for half in range(2):
                            cols = slice(512 * half, 512 * half + 512)
                            last = t_products(acc[:, 2 * t + half, :], hi, lo, k0 + kk, t, wh[:, kk, cols],
                                              wl[:, kk, cols], first and kk == 0, final and kk == 1)
                    return last

                def scores(c):
                    k0, nk = key_span(c)
                    for par in range(2):
                        if c == 0:
                            pe.wait_ge(*rope_read.at(l, 5 + par))
                        else:
                            pe.wait_ge(*score_read.at(l, 2 * c - 1 + par))
                        rows = slice(64 * par, 64 * par + 64)
                        for g in range(4):
                            last = mm(acc[:, par, g * P:g * P + nk],
                                      q_rows[rows, c, 2 * g * CHUNK:2 * (g + 1) * CHUNK],
                                      KT[rows, g, k0:k0 + nk], start=True, stop=True)
                        last.then_inc(scored.sem, 1)

                def turn_p(c):
                    for par in range(2):
                        if c == 0:
                            pe.wait_ge(*qk_done.at(l, 5 + par))
                        else:
                            pe.wait_ge(*pt_done.at(l, 2 * c - 1 + par))
                        pe.wait_ge(*p_done.at(l, c + 1))
                        for g in range(4):
                            last = nc.tensor.transpose(acc[:, 2 + par, g * P:g * P + P],
                                                       prob(c)[:, par, g, :], ident[:, :])
                        last.then_inc(p_turned.sem, 1)

                def pv_product(c):
                    dst = claim(l, "pv", c)
                    pe.wait_ge(*pt_done.at(l, 2 * c + 2))
                    v = VT[:, c // 2, :] if c in (0, 1, 3) else VS[:, :]
                    for par in range(2):
                        for g in range(4):
                            last = mm(dst[64 * par:64 * par + 64, g * P:g * P + P], v[:, 64 * g:64 * g + 64],
                                      prob_t(c)[:, 4 * par + g, :], start=True, stop=True)
                    last.then_inc(pv.sem, 1)

                def gates(c0, c1):
                    for c in range(c0, c1):
                        dst = claim(l, "gates", c)
                        pe.wait_ge(*uc_done.at(l, c + 1))
                        mm(dst[:, 0:S], bd_a[:, c, :], UC[:, c, :], start=True, stop=True)
                        mm(dst[:, S:2 * S], bd_x[:, c, :], UC[:, c, :], start=True, stop=True
                           ).then_inc(gates_mm.sem, 1)

                def turn_qk(m0, m1):
                    for m in range(m0, m1):
                        dst = bank("turn", m)
                        pe.wait_ge(*(rope_read.at(l, 3 + m) if m < 2 else qk_done.at(l, m - 1)))
                        pe.wait_ge(*roped.at(l, 6))
                        for k in range(4):
                            if m < 4:
                                t, h = m % 2, m // 2
                                src = QTOK[:, t, (4 * h + k) * P:(4 * h + k + 1) * P]
                            else:
                                src = KTOK[:, m - 4, k, :]
                            last = nc.tensor.transpose(dst[:, k * P:k * P + P], src, ident[:, :])
                        last.then_inc(qk_turned.sem, 1)

                def turn_m(c, t):
                    dst = claim(l, "turn_m", 2 * c + t)
                    pe.wait_ge(*m_done.at(l, 2 * c + t + 1))
                    for k in range(4):
                        last = nc.tensor.transpose(dst[:, k * P:k * P + P],
                                                   merged[:, t, 512 * c + k * P:512 * c + k * P + P], ident[:, :])
                    last.then_inc(m_turned.sem, 1)

                def turn_f(c):
                    for t in range(NT):
                        nk = 4 if c < GROUPS else 2
                        if nk == 4 or t == 0:
                            dst = claim(l, "turn_f", 2 * c + t)
                        pe.wait_ge(*f_up.at(l, 2 * c + t + 1))
                        for k in range(nk):
                            col = (k + (t * nk if nk == 2 else 0)) * P
                            last = nc.tensor.transpose(dst[:, col:col + P],
                                                       f_prod_t[:, 2 * (c % 2) + t, k * P:k * P + P], ident[:, :])
                        if nk == 4 or t == 1:
                            last.then_inc(f_turned.sem, 1)

                def down_panel(j, t, first, final):
                    c = j // 2
                    if t == 0:
                        split_ready(AT["down", j])
                        pe.wait_ge(*f_done.at(l, min(2 * c + 2, 2 * GROUPS + 1)))
                    return row_panel(AT["down", j], 4 * (c % 2) + 2 * (j % 2), z_hi, z_lo, t, first, final)

                for t in range(NT):
                    pe.wait_ge(vec_copied, 1)
                    pe.wait_ge(*xa_done.at(l, 2 * t + 2))
                    tile_pass(t, [("kv", 0, acc[:, 2 * t, :]), ("q0", 0, acc[:, 2 * t + 1, :])], xn_hi, xn_lo,
                              (lambda: turn_x(l, 0, "xn", 1)) if t == 0 else None)
                f_product("u", 0, xn_hi, xn_lo)
                f_product("u", 1, xn_hi, xn_lo)
                pe.wait_ge(*bd_loaded.at(l, 64))
                for j in range(2, 4):
                    f_product("u", j, xn_hi, xn_lo)
                    gates(2 * j - 4, 2 * j - 2)
                pe.wait_ge(*rope_read.at(l, 2))
                for j in range(2):
                    t_product("q1", j, [acc[:, 0, :], acc[:, 1, :]], xn_hi, xn_lo)
                    gates(4 + 2 * j, 6 + 2 * j)
                t_pair("gate_a", 0, xn_hi, xn_lo)
                turn_qk(0, 2)
                t_pair("gate_a", 1, xn_hi, xn_lo, between=lambda: turn_qk(2, 4))
                turn_qk(4, 6)
                f_product("gelu", 0, xn_hi, xn_lo)
                pe.wait_ge(*qk_done.at(l, 6))
                scores(0)
                f_product("gelu", 1, xn_hi, xn_lo)
                f_product("gelu", 2, xn_hi, xn_lo)
                scores(1)
                f_product("gelu", 3, xn_hi, xn_lo)
                turn_p(0)
                t_pair("gate_b", 0, xn_hi, xn_lo, between=lambda: scores(2))
                turn_p(1)
                t_pair("gate_b", 1, xn_hi, xn_lo, between=lambda: scores(3))
                turn_p(2)
                pv_product(0)
                pv_product(1)
                pe.wait_ge(*z_lo_done.at(l, 4))
                t_pair("pa", 0, z_hi, z_lo, between=lambda: turn_p(3))
                pv_product(2)
                pv_product(3)
                t_pair("pa", 1, z_hi, z_lo)
                pe.wait_ge(*o_done.at(l, 4))
                t_pair("pb", 0, xn_hi, xn_lo)
                for t in range(NT):
                    tile_pass(t, [("pb", 2, claim(l, "pb", 2 + t)[:, :])], xn_hi, xn_lo)
                    turn_m(t, 0)
                    if t == 0:
                        turn_m(0, 1)
                pe.wait_ge(*score_read.at(l, 8))
                pe.wait_ge(*pt_done.at(l, 8))
                for t in range(NT):
                    for j in range(4):
                        n = AT["wo", j]
                        if t == 0:
                            split_ready(n)
                            pe.wait_ge(*m_lo_done.at(l, 1 + 2 * (j // 2)))
                            if j == 2:
                                turn_m(1, 1)
                        elif j == 3:
                            turn_x(l, 4, "h", 0)
                        if t == 1 and j == 0:
                            pe.wait_ge(*m_lo_done.at(l, 4))
                        last = row_panel(n, 2 * j, z_hi, z_lo, t, j == 0, j == 3)
                        if t == NT - 1:
                            last.then_inc(panel_used.sem, 1)
                        elif j == 3:
                            last.then_inc(tile0.sem, 1)
                for t in range(NT):
                    pe.wait_ge(*xa_done.at(l, 6 + 2 * t))
                    dsts = [claim(l, name, t)[:, :] for name in ("fg", "fu")]
                    tile_pass(t, [("fg", 0, dsts[0]), ("fu", 0, dsts[1])], xn_hi, xn_lo,
                              (lambda: turn_x(l, 4, "h", 1)) if t == 0 else None)
                for c in range(1, GROUPS):
                    t_pair("fg", c, xn_hi, xn_lo)
                    t_pair("fu", c, xn_hi, xn_lo, between=lambda: turn_f(c - 1))
                    if c == 1:
                        pe.wait_ge(*branch_read.at(l, 2))
                    for j in (2 * c - 2, 2 * c - 1):
                        if j == 2 * GROUPS - 3:
                            continue
                        for t in range(NT):
                            last = down_panel(j, t, j == 0, False)
                        last.then_inc(panel_used.sem, 1)
                t_pair("fgu", 0, xn_hi, xn_lo, between=lambda: turn_f(GROUPS - 1))
                end = 2 * GROUPS
                for t in range(NT):
                    for j in range(end - 3, end + 1):
                        if t == 0 and j == end - 1:
                            turn_f(GROUPS)
                        if t == 1 and j == end and not last_layer:
                            turn_x(l + 1, 0, "xn", 0)
                        last = down_panel(j, t, False, j == end)
                        if t == NT - 1:
                            last.then_inc(panel_used.sem, 1)
                        elif j == end:
                            last.then_inc(tile0.sem, 1)

            for_layers(pe, layer)

        @block.scalar
        def _(act):
            step = [0]

            def own(ins):
                step[0] += 1
                ins.then_inc(act_step, 1)
                act.wait_ge(act_step, step[0])

            activate = nc.scalar.activation

            act.dma_start(pos_i[:, :], positions.rearrange("a (t p) -> p (a t)", p=P),
                          allow_slow_non_contiguous=True).then_inc(pos_loaded, 16)
            act.dma_start(sink_rows[:, :, :], attn_sinks.rearrange("l h -> (l h)").partition_broadcast(P)
                          .rearrange("p (l h) -> p l h", l=DEPTH)).then_inc(sinks_loaded, 16)

            def signalled(ins, sem, value):
                ins.then_inc(sem, 1)
                act.wait_ge(sem, value)

            def split_hi(l, n):
                act.wait_ge(*raw_loaded[n % RAW].at(l, LOADED[n]))
                activate(w_hi[:, SLOT[n], :], raw[:, n % RAW, :], ACT.Copy).then_inc(hi_done.sem, 1)

            def mean_square(n, src, sem, value):
                signalled(activate(junk[:, :], src, ACT.Square, scale=D ** -0.5,
                                   accum_out=mean_sq[:, n:n + 1]), sem, value)

            def xa_hi(l, first, name, t):
                for h in range(2):
                    m = first + 2 * t + h + 1
                    act.wait_ge(*turned.at(l, m))
                    activate(xn_hi[:, 4 * h:4 * h + 4, P * t:P * t + P],
                             bank(name, 2 * t + h)[:, :].rearrange("p (k s) -> p k s", k=4), ACT.Copy
                             ).then_inc(xa_hi_done.sem, 1)

            act.wait_ge(x_loaded[0], 16)
            mean_square(0, xres[:, 0, :], ms_done.sem, 1)
            xa_hi(0, 0, "xn", 0)
            split_hi(0, 0)
            act.wait_ge(x_loaded[1], 16)
            mean_square(1, xres[:, 1, :], ms_done.sem, 2)
            act.wait_ge(exp_ready, 1)
            activate(sp_t[:, :, :], sp_s[:, :, :], ACT.Exp, scale=-1.0).then_inc(exp_done, 1)
            for n in range(1, 4):
                split_hi(0, n)
            xa_hi(0, 0, "xn", 1)
            act.wait_ge(sines_ready, 1)
            activate(sin[:, :, 0, :], ang[:, :, :], ACT.Sin, scale=-1.0)
            activate(sin[:, :, 1, :], ang[:, :, :], ACT.Sin)
            activate(cos[:, :, :], digit[0][:, :, :], ACT.Sin).then_inc(sines_done, 1)
            act.sem_clear(act_step)

            def layer(l, last_layer):
                step[0] = 0

                def done(ins, sig, n):
                    ins.then_inc(sig.sem, 1)

                def panels_hi(used):
                    for n in SPLIT_AT[used]:
                        act.wait_ge(*panel_used.at(l, used + 1))
                        split_hi(l, n)

                def norm(m, n, src):
                    mean_square(n, src, *ms_done.at(l, m))

                def used(name, j):
                    act.wait_ge(*panel_used.at(l, AT[name, j] + 1))
                    return bank(name, j)[:, :]

                def two(t, j):
                    return t[:, 2 * j:2 * j + 2, :]

                def pair(ps):
                    return ps.rearrange("p (k s) -> p k s", k=2)

                def four(ps):
                    return ps.rearrange("p (k s) -> p k s", k=4)

                def decay(half):
                    cs = range(4 * half, 4 * half + 4)
                    for c in cs:
                        ins = activate(AG[:, c, :], h_lru[:, c, :], ACT.Exp, scale=vec[:, 8, c:c + 1])
                    own(ins)
                    for c in cs:
                        ins = activate(h_lru[:, c, :], h_lru[:, c, :], ACT.Tanh, scale=vec[:, 9, c:c + 1])
                    done(ins, a_done, half + 1)

                def gates(c0, c1):
                    for c in range(c0, c1):
                        act.wait_ge(*gates_mm.at(l, c + 1))
                        ps = bank("gates", c)
                        activate(h_lru[:, c, :], ps[:, 0:S], ACT.Sigmoid, bias=vec[:, 5, c:c + 1])
                        done(activate(IG[:, c, :], ps[:, S:2 * S], ACT.Sigmoid, bias=vec[:, 6, c:c + 1]),
                             gates_done, c + 1)

                def qk_copy(m0, m1):
                    for m in range(m0, m1):
                        act.wait_ge(*qk_turned.at(l, m + 1))
                        ps, t, h = bank("turn", m), m % 2, m // 2
                        if m < 4:
                            src = ps.rearrange("p (k c s) -> p k c s", k=4, c=2)
                            dst = q_rows[:, 2 * t:2 * t + 2, :].rearrange(
                                "p c (k s) -> p k c s", s=CHUNK)[:, 4 * h:4 * h + 4, :, :]
                        else:
                            src = four(ps)
                            dst = KT[:, :, P * (m - 4):P * (m - 3)]
                        done(activate(dst, src, ACT.Copy), qk_done, m + 1)

                def gelu_square(j):
                    if j >= 2:
                        act.wait_ge(*z_lo_done.at(l, j - 1))
                    done(activate(GT[:, j % 2, :], used("gelu", j), ACT.Square,
                                  scale=GELU_CUBE ** 0.5), g_sq, j + 1)

                def gelu_tanh(j):
                    act.wait_ge(*g_in.at(l, j + 1))
                    done(activate(GT[:, j % 2, :], GT[:, j % 2, :], ACT.Tanh, scale=GELU_SCALE), g_th, j + 1)

                def multipliers():
                    for half in range(2):
                        act.wait_ge(*v_done.at(l, half + 1))
                        v = UC[:, 4 * half:4 * half + 4, :]
                        done(activate(v, v, ACT.Sqrt), mult_done, half + 1)

                def z_hi_part(j):
                    act.wait_ge(*z_done.at(l, j + 1))
                    done(activate(two(z_hi, j), pair(GT[:, j % 2, :]), ACT.Copy), z_hi_done, j + 1)

                def gate(name, c):
                    if name == "gate_a":
                        act.wait_ge(*qk_turned.at(l, 2 * c + 2))
                    for t in range(NT):
                        sig, n = multiplied(name, c, t)
                        act.wait_ge(*sig.at(l, n))
                        ps = bank(name, 2 * c + t)[:, :]
                        if name == "gate_a":
                            done(activate(thA[:, t, 512 * c:512 * c + 512], ps, ACT.Tanh, scale=0.5),
                                 gate_th, 2 * c + t + 1)
                        else:
                            done(activate(thB(c, t), pair(ps), ACT.Tanh, scale=0.5), gate_th, 2 * c + t + 5)

                def exps(c):
                    _, nk = key_span(c)
                    if c == 1:
                        act.wait_ge(*h_done.at(l, 2))
                    act.wait_ge(*bias_done.at(l, c + 1))
                    for par in range(2):
                        for g in range(4):
                            h = 4 * par + g
                            ins = activate(prob(c)[:, par, g, 0:nk], acc[:, par, g * P:g * P + nk], ACT.Exp,
                                           bias=sm[:, c, 1, h:h + 1], scale=HEAD_DIM ** -0.5,
                                           accum_out=sm[:, c, 2, h:h + 1])
                        done(ins, score_read, 2 * c + par + 1)
                    done(activate(sm[:, c, 3, :], sm[:, c, 0, :], ACT.Exp), sink_exp, c + 1)

                def p_copy(c):
                    act.wait_ge(*(h_done.at(l, 2) if c < 2 else pv.at(l, c - 1)))
                    for par in range(2):
                        act.wait_ge(*p_turned.at(l, 2 * c + par + 1))
                        done(activate(prob_t(c)[:, 4 * par:4 * par + 4, :], four(acc[:, 2 + par, :]), ACT.Copy),
                             pt_done, 2 * c + par + 1)

                def o_hi_part(c):
                    act.wait_ge(*pv.at(l, c + 1))
                    done(activate(xn_hi[:, :, CHUNK * c:CHUNK * c + CHUNK],
                                  bank("pv", c)[:, :].rearrange("p (k s) -> p k s", k=KD), ACT.Copy),
                         o_hi_done, c + 1)

                def m_hi_part(c, t):
                    act.wait_ge(*m_turned.at(l, 2 * c + t + 1))
                    done(activate(z_hi[:, 4 * c:4 * c + 4, P * t:P * t + P], four(bank("turn_m", 2 * c + t)[:, :]),
                                  ACT.Copy, scale=0.5), m_hi_done, 2 * c + t + 1)

                def silu_tanh(c, t):
                    name, width = ("fg", 512) if c < GROUPS else ("fgu", 256)
                    sig, n = multiplied(name, c % GROUPS if c < GROUPS else 0, t)
                    act.wait_ge(*sig.at(l, n))
                    if c:
                        act.wait_ge(*f_gate.at(l, 2 * c + t - 1))
                    ps = bank(name, 2 * c + t if c < GROUPS else t)[:, 0:width]
                    done(activate(f_th_t[:, t, 0:width], ps, ACT.Tanh, scale=0.5), f_th, 2 * c + t + 1)

                def f_hi_part(c):
                    if c < GROUPS:
                        for t in range(NT):
                            act.wait_ge(*f_turned.at(l, 2 * c + t + 1))
                            k = 4 * (c % 2)
                            done(activate(z_hi[:, k:k + 4, P * t:P * t + P], four(bank("turn_f", 2 * c + t)[:, :]),
                                          ACT.Copy, scale=0.5), f_hi_done, 2 * c + t + 1)
                    else:
                        act.wait_ge(*f_turned.at(l, 2 * c + 1))
                        k = 4 * (c % 2)
                        ps = bank("turn_f", 2 * c)[:, :].rearrange("p (t k s) -> p k t s", t=2, k=2)
                        done(activate(z_hi[:, k:k + 2, :].rearrange("p k (t s) -> p k t s", t=2), ps, ACT.Copy,
                                      scale=0.5), f_hi_done, 2 * c + 1)

                for n, (name, j) in enumerate(PLAN[:AT["down", 2 * GROUPS - 3]]):
                    if name == "u":
                        done(activate(two(U[:, :, CW - 1:], j), pair(used("u", j)), ACT.Copy), u_done, j + 1)
                    if name == "gelu":
                        gelu_square(j)
                    if (name, j) in (("gate_b", 1), ("gate_b", 3)):
                        gate("gate_b", j // 2)
                    if (name, j) == ("gate_b", 3):
                        o_hi_part(0)
                        o_hi_part(1)
                    if (name, j) == ("wo", 0):
                        act.wait_ge(*tile0.at(l, 4))
                        norm(1, 2, acc[:, 0:2, :].rearrange("p b f -> p (b f)"))
                    if (name, j) == ("wo", 1):
                        act.wait_ge(*x_done.at(l, 1))
                        norm(2, 3, xres[:, 0, :])
                    if (name, j) == ("wo", 2):
                        xa_hi(l, 4, "h", 0)
                    if (name, j) == ("wo", 3):
                        panels_hi(n - 1)
                        act.wait_ge(*panel_used.at(l, n + 1))
                        norm(3, 4, acc[:, 2:4, :].rearrange("p b f -> p (b f)"))
                        panels_hi(n)
                    if name == "fg" and j < 2:
                        silu_tanh(0, j)
                    elif name == "fg" and j % 2:
                        silu_tanh(j // 2, 0)
                        silu_tanh(j // 2, 1)
                    if name == "fu" and j % 2 == 0 and j or (name, j) == ("fgu", 0):
                        f_hi_part(j // 2 - 1 if name == "fu" else GROUPS - 1)
                    if name != "wo" or j < 2:
                        panels_hi(n)
                    if name == "gelu" and j or (name, j) == ("gate_b", 0):
                        z_hi_part((j - 1) % 4)
                    if name == "gelu":
                        gelu_tanh(j)
                    if name == "u" and j > 1:
                        gates(2 * j - 4, 2 * j - 2)
                    if (name, j) == ("q1", 0):
                        gates(4, 6)
                    if (name, j) == ("q1", 1):
                        gates(6, 8)
                        decay(0)
                    if (name, j) == ("gate_a", 0):
                        decay(1)
                    if (name, j) == ("gate_a", 1):
                        gate("gate_a", 0)
                        qk_copy(0, 2)
                    if (name, j) == ("gate_a", 2):
                        qk_copy(2, 4)
                        multipliers()
                    if (name, j) == ("gate_a", 3):
                        gate("gate_a", 1)
                        qk_copy(4, 6)
                    if (name, j) in SCORES_AT:
                        exps(SCORES_AT.index((name, j)))
                    if (name, j) == ("gelu", 3):
                        p_copy(0)
                    if (name, j) == ("gate_b", 1):
                        p_copy(1)
                    if (name, j) == ("gate_b", 3):
                        p_copy(2)
                    if (name, j) == ("pa", 0):
                        p_copy(3)
                    if (name, j) == ("pa", 1):
                        o_hi_part(2)
                    if (name, j) == ("pa", 2):
                        o_hi_part(3)
                    if (name, j) == ("pb", 1):
                        m_hi_part(0, 0)
                        m_hi_part(0, 1)
                    if (name, j) == ("pb", 3):
                        m_hi_part(1, 0)
                        m_hi_part(1, 1)
                    if (name, j) == ("wo", 3):
                        act.wait_ge(*x_done.at(l, 2))
                        norm(4, 5, xres[:, 1, :])
                        xa_hi(l, 4, "h", 1)
                silu_tanh(GROUPS, 0)
                silu_tanh(GROUPS, 1)
                f_hi_part(GROUPS)
                act.wait_ge(*tile0.at(l, 7))
                norm(5, 6, acc[:, 0:2, :].rearrange("p b f -> p (b f)"))

                def next_hi(n):
                    act.wait_ge(*panel_used.at(l, LAST_OF[n] + 1))
                    split_hi(l + 1, n)

                if not last_layer:
                    next_hi(0)
                    act.wait_ge(*x_done.at(l, 3))
                    norm(6, 0, xres[:, 0, :])
                    next_hi(1)
                    xa_hi(l + 1, 0, "xn", 0)
                act.wait_ge(*panel_used.at(l, NPAN))
                norm(6 if last_layer else 7, 7, acc[:, 2:4, :].rearrange("p b f -> p (b f)"))
                if not last_layer:
                    next_hi(2)
                    act.wait_ge(*x_done.at(l, 4))
                    norm(8, 1, xres[:, 1, :])
                    next_hi(3)
                    xa_hi(l + 1, 0, "xn", 1)
                    own(activate(idle[:, :], eps_t[:, :], ACT.Copy))
                    act.sem_clear(act_step)

            for_layers(act, layer)

        @block.vector
        def _(dve):
            v = nc.vector
            step = [0]

            def count(ins):
                step[0] += 1
                ins.then_inc(dve_step, 1)

            def own(ins):
                count(ins)
                dve.wait_ge(dve_step, step[0])

            def signalled(ins, sem, value):
                ins.then_inc(sem, 1)
                dve.wait_ge(sem, value)

            def split_lo(l, n):
                dve.wait_ge(*hi_done.at(l, n + 1))
                v.tensor_tensor(w_lo[:, SLOT[n], :], raw[:, n % RAW, :], bits(w_hi[:, SLOT[n], :]),
                                ALU.subtract).then_inc(split_done.sem, 1)

            def normed(l, column, ready, t, gains):
                dve.wait_ge(*ready)
                dve.wait_ge(*pre_loaded.at(l, 16 * gains))
                v.scalar_tensor_tensor(QTOK[:, t, :], xres[:, t, :], rstd[:, column:column + 1], g_pre[:, :],
                                       ALU.mult, ALU.mult).then_inc(xs_done.sem, 1)

            def xa_lo(l, first, name, t):
                for h in range(2):
                    m = first + 2 * t + h + 1
                    dve.wait_ge(*xa_hi_done.at(l, m))
                    cols = slice(P * t, P * t + P)
                    v.tensor_tensor(xn_lo[:, 4 * h:4 * h + 4, cols],
                                    bank(name, 2 * t + h)[:, :].rearrange("p (k s) -> p k s", k=4),
                                    bits(xn_hi[:, 4 * h:4 * h + 4, cols]), ALU.subtract).then_inc(xa_done.sem, 1)

            dve.wait_ge(pos_loaded, 16)
            v.tensor_copy(pos_f[:, :], pos_i[:, :]).then_inc(pos_done, 1)
            normed(0, 0, (rstd_done.sem, 1), 0, 1)
            xa_lo(0, 0, "xn", 0)
            split_lo(0, 0)
            dve.wait_ge(vec_turned, 1)
            taps = DEPTH * CW * KD
            v.tensor_copy(vecs[:, :, 0:CW, :], acc[:, 3, 0:taps].rearrange("p (l v k) -> p l v k", l=DEPTH, v=CW))
            signalled(v.tensor_copy(vecs[:, :, CW:8, :],
                                    acc[:, 3, taps:P].rearrange("p (v l k) -> p l v k", l=DEPTH, v=8 - CW)),
                      vec_copied, 1)
            lam = vecs[:, :, 7, :]
            own(v.tensor_scalar(sp_p[:, :, :], lam, -1.0, None, ALU.mult))
            v.tensor_tensor(sp_s[:, :, :], lam, sp_p[:, :, :], ALU.max).then_inc(exp_ready, 1)
            normed(0, 1, (rstd_done.sem, 2), 1, 1)
            dve.wait_ge(exp_done, 1)
            own(v.tensor_scalar(sp_s[:, :, :], sp_t[:, :, :], 2.0, None, ALU.add))
            own(v.reciprocal(sp_s[:, :, :], sp_s[:, :, :]))
            own(v.tensor_tensor(sp_s[:, :, :], sp_s[:, :, :], sp_t[:, :, :], ALU.mult))
            own(v.tensor_tensor(sp_t[:, :, :], sp_s[:, :, :], sp_s[:, :, :], ALU.mult))
            split_lo(0, 1)
            split_lo(0, 2)
            split_lo(0, 3)
            dve.wait_ge(angle_done, 1)
            own(v.tensor_scalar(ang[:, :, :], ang[:, :, :], 3.1415925, -3.1415925, ALU.min, ALU.max))
            own(v.tensor_scalar(digit[0][:, :, :], ang[:, :, :], -1.0, None, ALU.mult))
            own(v.tensor_tensor(digit[0][:, :, :], ang[:, :, :], digit[0][:, :, :], ALU.max))
            v.tensor_scalar(digit[0][:, :, :], digit[0][:, :, :], -1.0, float(np.pi / 2), ALU.mult,
                            ALU.add).then_inc(sines_ready, 1)
            xa_lo(0, 0, "xn", 1)
            own(v.tensor_scalar(sp_p[:, :, :], sp_t[:, :, :], 1.0 / 17, None, ALU.mult))
            for odd in range(15, 1, -2):
                own(v.scalar_tensor_tensor(sp_p[:, :, :], sp_p[:, :, :], 1.0 / odd, sp_t[:, :, :], ALU.add, ALU.mult))
            own(v.scalar_tensor_tensor(sp_p[:, :, :], sp_p[:, :, :], 1.0, sp_s[:, :, :], ALU.add, ALU.mult))
            own(v.tensor_scalar(sp_t[:, :, :], lam, -1.0, 0.0, ALU.mult, ALU.max))
            own(v.scalar_tensor_tensor(sp_p[:, :, :], sp_p[:, :, :], 2.0, sp_t[:, :, :], ALU.mult, ALU.add))
            own(v.tensor_scalar(vecs[:, :, 8, :], sp_p[:, :, :], -LRU_C, None, ALU.mult))
            own(v.tensor_scalar(vecs[:, :, 9, :], sp_p[:, :, :], LRU_C, None, ALU.mult))

            dve.wait_ge(sinks_loaded, 16)
            by_head = sink_rows[:, :, :].rearrange("p l (g i r) -> p l g i r", i=2, r=2)
            for i in range(2):
                for par in range(2):
                    rows = slice(64 * i, 64 * i + 64)
                    own(v.tensor_copy(sinks[rows, :, 0, 4 * par:4 * par + 4], by_head[rows, :, :, i, par]))
            own(v.tensor_scalar(sinks[:, :, 1, :], sinks[:, :, 0, :], -1.0, None, ALU.mult))
            dve.wait_ge(sines_done, 1)
            dve.sem_clear(dve_step)

            def layer(l, last_layer):
                step[0] = 0

                def done(ins, sig, n):
                    ins.then_inc(sig.sem, 1)

                def panels_lo(used):
                    for n in SPLIT_AT[used]:
                        split_lo(l, n)

                def norm(m, column, t, gains):
                    normed(l, column, rstd_done.at(l, m), t, gains)

                def two(t, j):
                    return t[:, 2 * j:2 * j + 2, :]

                def pair(ps):
                    return ps.rearrange("p (k s) -> p k s", k=2)

                def conv(j):
                    dve.wait_ge(*tap_done.at(l, 2 * j + 2))
                    for k in range(1, CW):
                        for c in (2 * j, 2 * j + 1):
                            if k > 1:
                                dve.wait_ge(dve_step, step[0] - (k < CW - 1 or c % 2 == 0))
                            ins = v.scalar_tensor_tensor(UC[:, c, :], U[:, c, k:k + S], vec[:, k, c:c + 1],
                                                         UC[:, c, :], ALU.mult, ALU.add)
                            if k < CW - 1:
                                count(ins)
                            else:
                                done(ins, uc_done, c + 1)

                def rope(name, t):
                    n = {"kv": 1, "q0": 2}[name] + 2 * t if name != "q1" else 5 + t
                    b = t if name == "q1" else 2 * t + (name == "q0")
                    heads = 4 if name == "kv" else 8
                    width = heads * HEAD_DIM
                    ps = acc[:, b, 0:width]
                    sig, m = multiplied(name, 0, t)
                    dve.wait_ge(*sig.at(l, m))
                    if n > 1:
                        dve.wait_ge(*roped.at(l, n - 1))
                    halves = ps.rearrange("p (h i d) -> p h i d", i=2, d=32)
                    c2 = cos[:, t, :].unsqueeze(1).broadcast_to([P, 2 * heads, 32])
                    t1 = GT[:, 0, 0:width]
                    t2 = GT[:, 1, 0:width].rearrange("p (h i d) -> p h i d", i=2, d=32)
                    v.tensor_tensor(t1.rearrange("p (h d) -> p h d", d=32), ps.rearrange("p (h d) -> p h d", d=32),
                                    c2, ALU.mult)
                    for i in range(2):
                        s2 = sin[:, t, i, :].unsqueeze(1).broadcast_to([P, heads, 32])
                        ins = v.tensor_tensor(t2[:, :, i, :], halves[:, :, 1 - i, :], s2, ALU.mult)
                    if name == "kv":
                        v.tensor_copy(VT[:, t, :], acc[:, b, 256:512])
                        src, dst = (64, 0) if t == 0 else (0, 64)
                        ins = v.tensor_copy(VS[dst:dst + 64, :], acc[src:src + 64, b, 256:512])
                    done(ins, rope_read, n)
                    dve.wait_ge(*rope_read.at(l, n))
                    if name == "kv":
                        for copy in range(2):
                            ins = v.tensor_tensor(KTOK[:, t, :, 64 * copy:64 * copy + 64],
                                                  t1.rearrange("p (h d) -> p h d", d=64),
                                                  GT[:, 1, 0:width].rearrange("p (h d) -> p h d", d=64), ALU.add)
                    else:
                        q = 512 * (name == "q1")
                        ins = v.tensor_tensor(QTOK[:, t, q:q + 512], t1, GT[:, 1, :], ALU.add)
                    done(ins, roped, n)

                def lru_v(half):
                    cs = slice(4 * half, 4 * half + 4)
                    dve.wait_ge(*a_done.at(l, half + 1))
                    own(v.tensor_tensor(IG[:, cs, :], IG[:, cs, :], UC[:, cs, :], ALU.mult))
                    own(v.tensor_tensor(UC[:, cs, :], AG[:, cs, :], AG[:, cs, :], ALU.mult))
                    done(v.scalar_tensor_tensor(UC[:, cs, :], UC[:, cs, :], 1.0, h_lru[:, cs, :],
                                                ALU.add, ALU.mult), v_done, half + 1)

                def lru_scan(half):
                    cs = slice(4 * half, 4 * half + 4)
                    dve.wait_ge(*mult_done.at(l, half + 1))
                    own(v.tensor_tensor(IG[:, cs, :], IG[:, cs, :], UC[:, cs, :], ALU.mult))
                    for c in range(4 * half, 4 * half + 4):
                        ins = v.tensor_tensor_scan(h_lru[:, c, :], AG[:, c, :], IG[:, c, :], 0.0, ALU.mult, ALU.add)
                    done(ins, h_done, half + 1)

                def gelu_inner(j):
                    dve.wait_ge(*g_sq.at(l, j + 1))
                    g = GT[:, j % 2, :]
                    done(v.scalar_tensor_tensor(g, g, 1.0, bank("gelu", j)[:, :], ALU.add, ALU.mult), g_in, j + 1)

                def gelu_outer(j):
                    dve.wait_ge(*g_th.at(l, j + 1))
                    g = GT[:, j % 2, :]
                    done(v.scalar_tensor_tensor(g, g, 1.0, bank("gelu", j)[:, :], ALU.add, ALU.mult), g_read, j + 1)

                def z_part(j):
                    dve.wait_ge(*g_read.at(l, j + 1))
                    g = pair(GT[:, j % 2, :])
                    done(v.scalar_tensor_tensor(g, g, 0.5, two(h_lru, j), ALU.mult, ALU.mult), z_done, j + 1)

                def z_lo_part(j):
                    dve.wait_ge(*z_hi_done.at(l, j + 1))
                    done(v.tensor_tensor(two(z_lo, j), pair(GT[:, j % 2, :]), bits(two(z_hi, j)), ALU.subtract),
                         z_lo_done, j + 1)

                def score_max(c):
                    _, nk = key_span(c)
                    if c == 0:
                        own(v.memset(prob(c)[:, :, :, nk:], 0.0))
                    dve.wait_ge(*scored.at(l, 2 * c + 2))
                    both = acc[:, 0:2, :].rearrange("p r (g k) -> p r g k", g=4)[:, :, :, 0:nk]
                    own(v.tensor_reduce(sm[:, c, 0, :].rearrange("p (r g) -> p r g", r=2), both, AX.X, ALU.max))
                    own(v.scalar_tensor_tensor(sm[:, c, 1, :], sm[:, c, 0, :], -HEAD_DIM ** -0.5, sink[:, 1, :],
                                               ALU.mult, ALU.min))
                    done(v.tensor_tensor(sm[:, c, 0, :], sink[:, 0, :], sm[:, c, 1, :], ALU.add), bias_done, c + 1)

                def softmax(c):
                    _, nk = key_span(c)
                    dve.wait_ge(*sink_exp.at(l, c + 1))
                    own(v.tensor_tensor(sm[:, c, 4, :], sm[:, c, 2, :], sm[:, c, 3, :], ALU.add))
                    own(v.reciprocal(sm[:, c, 5, :], sm[:, c, 4, :]))
                    inv = sm[:, c, 5, :].rearrange("p (r g) -> p r g", r=2).unsqueeze(3)
                    p = prob(c)[:, :, :, 0:nk]
                    done(v.tensor_tensor(p, p, inv.broadcast_to([P, 2, 4, nk]), ALU.mult), p_done, c + 1)

                def o_lo_part(c):
                    dve.wait_ge(*o_hi_done.at(l, c + 1))
                    cols = slice(CHUNK * c, CHUNK * c + CHUNK)
                    done(v.tensor_tensor(xn_lo[:, :, cols], bank("pv", c)[:, :].rearrange("p (k s) -> p k s", k=KD),
                                         bits(xn_hi[:, :, cols]), ALU.subtract), o_done, c + 1)

                def add_branch(m, n, i, t, gains):
                    dve.wait_ge(*rstd_done.at(l, m))
                    dve.wait_ge(*post_loaded.at(l, 16 * gains))
                    tmp = QT[:, 4 * t:4 * t + 4, :].rearrange("p k s -> p (k s)")
                    done(v.scalar_tensor_tensor(tmp, acc[:, 2 * t:2 * t + 2, :].rearrange("p b f -> p (b f)"),
                                                rstd[:, n:n + 1], g_post[:, :], ALU.mult, ALU.mult), branch_read, i)
                    dve.wait_ge(*branch_read.at(l, i))
                    done(v.tensor_tensor(xres[:, t, :], xres[:, t, :], tmp, ALU.add), x_done, i)

                def four(ps):
                    return ps.rearrange("p (k s) -> p k s", k=4)

                def branch_a(c):
                    for t in range(NT):
                        dve.wait_ge(*gate_th.at(l, 2 * c + t + 1))
                        sig, n = multiplied("pa", c, t)
                        dve.wait_ge(*sig.at(l, n))
                        cols = slice(512 * c, 512 * c + 512)
                        done(v.scalar_tensor_tensor(merged[:, t, cols], thA[:, t, cols], 1.0,
                                                    bank("pa", 2 * c + t)[:, :], ALU.add, ALU.mult),
                             ya_read, 2 * c + t + 1)

                def branch_b(c, t):
                    dve.wait_ge(*gate_th.at(l, 2 * c + t + 5))
                    sig, n = multiplied("pb", c, t)
                    dve.wait_ge(*sig.at(l, n))
                    cols = slice(512 * c, 512 * c + 512)
                    done(v.scalar_tensor_tensor(pair(GT[:, t, :]), thB(c, t), 1.0, pair(bank("pb", 2 * c + t)[:, :]),
                                                ALU.add, ALU.mult), yb_read, 2 * c + t + 1)
                    dve.wait_ge(*yb_read.at(l, 2 * c + t + 1))
                    done(v.tensor_tensor(merged[:, t, cols], merged[:, t, cols], GT[:, t, :], ALU.add),
                         m_done, 2 * c + t + 1)

                def m_lo_part(c, t):
                    dve.wait_ge(*m_hi_done.at(l, 2 * c + t + 1))
                    ks, cols = slice(4 * c, 4 * c + 4), slice(P * t, P * t + P)
                    done(v.scalar_tensor_tensor(z_lo[:, ks, cols], four(bank("turn_m", 2 * c + t)[:, :]), 0.5,
                                                bits(z_hi[:, ks, cols]), ALU.mult, ALU.subtract),
                         m_lo_done, 2 * c + t + 1)

                def silu(c, t):
                    if c:
                        dve.wait_ge(*f_up.at(l, 2 * c + t - 1))
                    dve.wait_ge(*f_th.at(l, 2 * c + t + 1))
                    ps = bank("fg", 2 * c + t)[:, :] if c < GROUPS else bank("fgu", t)[:, 0:256]
                    w = 512 if c < GROUPS else 256
                    done(v.scalar_tensor_tensor(f_silu_t[:, t, 0:w], f_th_t[:, t, 0:w], 1.0, ps, ALU.add, ALU.mult),
                         f_gate, 2 * c + t + 1)

                def f_product(c, t):
                    if c < GROUPS:
                        sig, n = multiplied("fu", c, t)
                        dve.wait_ge(*sig.at(l, n))
                        ps, w = bank("fu", 2 * c + t)[:, :], 512
                    else:
                        ps, w = bank("fgu", t)[:, 256:512], 256
                    dve.wait_ge(*f_gate.at(l, 2 * c + t + 1))
                    done(v.tensor_tensor(f_prod_t[:, 2 * (c % 2) + t, 0:w], f_silu_t[:, t, 0:w], ps, ALU.mult),
                         f_up, 2 * c + t + 1)

                def f_lo_part(c):
                    k = 4 * (c % 2)
                    if c < GROUPS:
                        for t in range(NT):
                            dve.wait_ge(*f_hi_done.at(l, 2 * c + t + 1))
                            cols = slice(P * t, P * t + P)
                            done(v.scalar_tensor_tensor(z_lo[:, k:k + 4, cols], four(bank("turn_f", 2 * c + t)[:, :]),
                                                        0.5, bits(z_hi[:, k:k + 4, cols]), ALU.mult, ALU.subtract),
                                 f_done, 2 * c + t + 1)
                        return
                    dve.wait_ge(*f_hi_done.at(l, 2 * c + 1))
                    ps = bank("turn_f", 2 * c)[:, :].rearrange("p (t k s) -> p t k s", t=2, k=2)
                    for t in range(NT):
                        cols = slice(P * t, P * t + P)
                        ins = v.scalar_tensor_tensor(z_lo[:, k:k + 2, cols], ps[:, t, :, :], 0.5,
                                                     bits(z_hi[:, k:k + 2, cols]), ALU.mult, ALU.subtract)
                        if t == 0:
                            own(ins)
                    done(ins, f_done, 2 * c + 1)

                own(v.tensor_copy(vec[:, :, :], vecs[:, bass.ds(l, 1), :, :].rearrange("p o v k -> p (o v) k")))
                own(v.tensor_copy(sink[:, :, :], sinks[:, bass.ds(l, 1), :, :].rearrange("p o n h -> p (o n) h")))

                for n, (name, j) in enumerate(PLAN[:AT["down", 2 * GROUPS - 3]]):
                    if (name, j) == ("kv", 0):
                        rope("kv", 0)
                    if (name, j) == ("kv", 1):
                        rope("kv", 1)
                    if name == "gelu":
                        gelu_inner(j)
                    if name == "gelu" and j or (name, j) == ("gate_b", 0):
                        z_part((j - 1) % 4)
                    if (name, j) in SCORES_AT:
                        score_max(SCORES_AT.index((name, j)))
                    if (name, j) in SOFTMAX_AT:
                        softmax(SOFTMAX_AT.index((name, j)))
                    if name == "pa" and j % 2:
                        branch_a(j // 2)
                    if (name, j) == ("pb", 1):
                        branch_b(0, 0)
                        branch_b(0, 1)
                    if (name, j) == ("pb", 2):
                        branch_b(1, 0)
                    if (name, j) == ("pb", 3):
                        branch_b(1, 1)
                    if (name, j) == ("wo", 0):
                        add_branch(1, 2, 1, 0, 1)
                    if (name, j) == ("wo", 1):
                        norm(2, 3, 0, 2)
                        xa_lo(l, 4, "h", 0)
                    if (name, j) == ("wo", 3):
                        add_branch(3, 4, 2, 1, 1)
                        panels_lo(n - 1)
                    if name == "fg" and j < 2:
                        silu(0, j)
                        if j == 0:
                            f_product(0, 0)
                    elif name == "fg" and j % 2:
                        silu(j // 2, 0)
                        silu(j // 2, 1)
                    if (name, j) == ("fu", 1):
                        f_product(0, 1)
                    elif name == "fu" and j % 2:
                        f_product(j // 2, 0)
                        f_product(j // 2, 1)
                    if name == "fu" and j % 2 == 0 and j or (name, j) == ("fgu", 0):
                        f_lo_part(j // 2 - 1 if name == "fu" else GROUPS - 1)
                    if name != "wo" or j < 2:
                        panels_lo(n)
                    if (name, j) == ("kv", 0):
                        rope("q0", 0)
                    if name == "u":
                        conv(j)
                    if (name, j) == ("q0", 1):
                        rope("q0", 1)
                    if (name, j) == ("q1", 1):
                        rope("q1", 0)
                        rope("q1", 1)
                    if (name, j) == ("gate_a", 0):
                        lru_v(0)
                    if (name, j) == ("gate_a", 1):
                        lru_v(1)
                    if (name, j) == ("gate_a", 2):
                        lru_scan(0)
                    if (name, j) == ("gate_a", 3):
                        lru_scan(1)
                    if name == "gelu":
                        if j:
                            z_lo_part(j - 1)
                        gelu_outer(j)
                    if (name, j) == ("gate_b", 0):
                        z_lo_part(3)
                    if (name, j) == ("gate_b", 3):
                        o_lo_part(0)
                        o_lo_part(1)
                    if (name, j) == ("pa", 1):
                        o_lo_part(2)
                    if (name, j) == ("pa", 2):
                        o_lo_part(3)
                    if (name, j) == ("pb", 1):
                        m_lo_part(0, 0)
                        m_lo_part(0, 1)
                    if (name, j) == ("pb", 3):
                        m_lo_part(1, 0)
                        m_lo_part(1, 1)
                    if (name, j) == ("wo", 3):
                        norm(4, 5, 1, 2)
                        panels_lo(n)
                        xa_lo(l, 4, "h", 1)
                for t in range(NT):
                    silu(GROUPS, t)
                    f_product(GROUPS, t)
                f_lo_part(GROUPS)
                add_branch(5, 6, 3, 0, 2)
                if not last_layer:
                    split_lo(l + 1, 0)
                    normed(l + 1, 0, rstd_done.at(l, 6), 0, 1)
                    xa_lo(l + 1, 0, "xn", 0)
                    split_lo(l + 1, 1)
                add_branch(6 if last_layer else 7, 7, 4, 1, 2)
                if not last_layer:
                    split_lo(l + 1, 2)
                    normed(l + 1, 1, rstd_done.at(l, 8), 1, 1)
                    split_lo(l + 1, 3)
                    xa_lo(l + 1, 0, "xn", 1)
                    own(v.tensor_copy(sm[:, 0, 5, 0:1], eps_t[:, :]))
                    dve.sem_clear(dve_step)

            for_layers(dve, layer)


INS = ["x", "positions", "pre_mix_g", "w_in", "conv_w", "conv_b", "lru_wa", "lru_ba", "lru_wx", "lru_bx",
       "lru_lambda", "attn_sinks", "w_pa", "w_pb", "w_o", "post_mix_g", "pre_ffn_g", "w_ffn_gate",
       "w_ffn_up", "w_ffn_down", "post_ffn_g"]


def kernel(**inputs):
    import concourse.bacc as bacc
    from concourse.bass_utils import run_bass_kernel_spmd

    nc = bacc.Bacc("TRN2", target_bir_lowering=False, num_devices=1)
    arrays, args = {}, []
    for name in INS:
        a = np.ascontiguousarray(inputs[name])
        arrays[f"in_{name}"] = a
        args.append(nc.dram_tensor(f"in_{name}", a.shape, mybir.dt.from_np(a.dtype), kind="ExternalInput").ap())
    shape = inputs["x"].shape
    args.append(nc.dram_tensor("out_0", shape, F32, kind="ExternalOutput").ap())
    trunk(nc, *args)
    result = run_bass_kernel_spmd(nc, [arrays], core_ids=[0])
    return result.results[0]["out_0"]
```
